# Optimizing a Trainium2 kernel written in Bass

```python
import math
import jax, jax.numpy as jnp
from jax import lax
import numpy as np

D_MODEL = 2048
BATCH = 1
SEQ = 512
DEPTH = 1

GRID_W = 64
CTX_LEN = 256
MIX_WIDTH = D_MODEL
HG_WIDTH = MIX_WIDTH // 2
DA_WIDTH = MIX_WIDTH - HG_WIDTH
HG_EXPAND = 128
HG_HEADS = HG_WIDTH // HG_EXPAND
HG_CHUNK = 64
DA_HEAD_DIM = 64
DA_V_DIM = 2 * DA_HEAD_DIM
DA_HEADS = DA_WIDTH // DA_V_DIM
Q_BLOCK = 128
ROPE_BASE = 10000.0
PEER_HEADS = 8
PEER_NKEYS = 128
PEER_EXPERTS = PEER_NKEYS * PEER_NKEYS
PEER_QDIM = 256
PEER_TOPK = 16
PEER_BLOCK = 128
RMS_EPS = 1e-6
IN_WIDTHS = (HG_WIDTH,) * 5 + (DA_WIDTH,) * 3
IN_COLS = sum(IN_WIDTHS)
IN_SPLITS = tuple(int(s) for s in np.cumsum(IN_WIDTHS)[:-1])

kernel_name = 'hybrid_hgrn2_diffattn_peer_block'

F32 = jnp.float32

def rmsnorm(x, g):
    xf = x.astype(F32)
    y = xf * lax.rsqrt(jnp.mean(xf * xf, axis=-1, keepdims=True) + RMS_EPS)
    return (y * g.astype(F32)).astype(x.dtype)

def split_heads(t, n_heads):
    b, s, _ = t.shape
    return t.reshape(b, s, n_heads, -1).transpose(0, 2, 1, 3)

def merge_heads(t):
    b, h, s, d = t.shape
    return t.transpose(0, 2, 1, 3).reshape(b, s, h * d)

def flip_seq(t):
    return jnp.flip(t, axis=2)

def rope_1d(t, ang):
    half = t.shape[-1] // 2
    cos = jnp.cos(ang).astype(t.dtype)
    sin = jnp.sin(ang).astype(t.dtype)
    t1, t2 = t[..., :half], t[..., half:]
    return jnp.concatenate([t1 * cos - t2 * sin, t1 * sin + t2 * cos], axis=-1)

def axial_rope(t, ang_row, ang_col):
    half = t.shape[-1] // 2
    return jnp.concatenate([rope_1d(t[..., :half], ang_row), rope_1d(t[..., half:], ang_col)], axis=-1)

def chunk_recurrence(q, k, v, log_f, s0, with_output):
    b, h, t, dk = k.shape
    dv = v.shape[-1]
    n = t // HG_CHUNK

    def to_chunks(z):
        return z.reshape(b, h, n, HG_CHUNK, z.shape[-1]).transpose(2, 0, 1, 3, 4)

    mask = jnp.tril(jnp.ones((HG_CHUNK, HG_CHUNK), dtype=bool))[:, :, None]

    def step(state, inp):
        kc, vc, lfc = inp[0], inp[1], inp[2]
        cum = jnp.cumsum(lfc, axis=-2)
        last = cum[..., -1:, :]
        new_state = (jnp.exp(last[..., 0, :])[..., None] * state
                     + jnp.einsum('bhsk,bhsv->bhkv', kc * jnp.exp(last - cum), vc))
        if not with_output:
            return new_state, None
        qc = inp[3]
        diff = cum[..., :, None, :] - cum[..., None, :, :]
        decay = jnp.where(mask, jnp.exp(jnp.where(mask, diff, 0.0)), 0.0)
        scores = jnp.einsum('bhtk,bhtsk,bhsk->bhts', qc, decay, kc)
        out = (jnp.einsum('bhtk,bhkv->bhtv', qc * jnp.exp(cum), state)
               + jnp.einsum('bhts,bhsv->bhtv', scores, vc))
        return new_state, out

    inputs = (k, v, log_f) + ((q,) if with_output else ())
    final, outs = lax.scan(step, s0, tuple(to_chunks(z) for z in inputs))
    if with_output:
        outs = outs.transpose(1, 2, 0, 3, 4).reshape(b, h, t, dv)
    return outs, final

def hgrn2_mixer(lat_parts, ctx_parts, lb, norm_g, with_ctx_out):
    dtype = lat_parts[0].dtype
    lb = lb.reshape(2, HG_HEADS, 1, HG_EXPAND)

    def gates(z, lb_dir):
        f = lb_dir + (1.0 - lb_dir) * jax.nn.sigmoid(split_heads(z.astype(F32), HG_HEADS))
        return 1.0 - f, jnp.log(f)

    def readout(o, g):
        o = o * lax.rsqrt(jnp.mean(o * o, axis=-1, keepdims=True) + RMS_EPS)
        o = o * norm_g.astype(F32).reshape(HG_HEADS, 1, HG_EXPAND)
        return merge_heads(o * jax.nn.silu(split_heads(g.astype(F32), HG_HEADS))).astype(dtype)

    def scan_both(parts, s_fwd, s_bwd, with_out):
        q, zf, zb, i = parts[0], parts[1], parts[2], parts[3]
        qh = jax.nn.silu(split_heads(q.astype(F32), HG_HEADS)) if with_out else None
        ih = split_heads(i.astype(F32), HG_HEADS)
        kf, lff = gates(zf, lb[0])
        kb, lfb = gates(zb, lb[1])
        o_f, st_f = chunk_recurrence(qh, kf, ih, lff, s_fwd, with_out)
        o_b, st_b = chunk_recurrence(flip_seq(qh) if with_out else None, flip_seq(kb), flip_seq(ih),
                                     flip_seq(lfb), s_bwd, with_out)
        o = o_f + flip_seq(o_b) if with_out else None
        return o, st_f, st_b

    b = lat_parts[0].shape[0]
    s0 = jnp.zeros((b, HG_HEADS, HG_EXPAND, HG_EXPAND), F32)
    o_ctx, st_f, st_b = scan_both(ctx_parts, s0, s0, with_ctx_out)
    o_lat, _, _ = scan_both(lat_parts, st_f, st_b, True)
    out_lat = readout(o_lat, lat_parts[4])
    out_ctx = readout(o_ctx, ctx_parts[4]) if with_ctx_out else None
    return out_lat, out_ctx

def diff_attend(q1, q2, k1, k2, v, lam):
    scale = DA_HEAD_DIM ** -0.5
    p1 = jax.nn.softmax(jnp.einsum('bhqd,bhkd->bhqk', q1, k1).astype(F32) * scale, axis=-1)
    p2 = jax.nn.softmax(jnp.einsum('bhqd,bhkd->bhqk', q2, k2).astype(F32) * scale, axis=-1)
    return jnp.einsum('bhqk,bhkv->bhqv', (p1 - lam * p2).astype(v.dtype), v)

def diff_attention(lat_parts, ctx_parts, lam, lam_init, subln_g, ang_row, ang_col, with_ctx_out):

    def heads(q, k, v):
        b, t, _ = q.shape
        q = q.reshape(b, t, DA_HEADS, 2, DA_HEAD_DIM).transpose(3, 0, 2, 1, 4)
        k = k.reshape(b, t, DA_HEADS, 2, DA_HEAD_DIM).transpose(3, 0, 2, 1, 4)
        return q[0], q[1], k[0], k[1], split_heads(v, DA_HEADS)

    def subln(o):
        of = o.astype(F32)
        of = of * lax.rsqrt(jnp.mean(of * of, axis=-1, keepdims=True) + RMS_EPS)
        of = of * subln_g.astype(F32).reshape(DA_HEADS, 1, DA_V_DIM) * (1.0 - lam_init)
        return merge_heads(of).astype(o.dtype)

    lq1, lq2, lk1, lk2, lv = heads(*lat_parts)
    lq1, lq2, lk1, lk2 = [axial_rope(z, ang_row, ang_col) for z in (lq1, lq2, lk1, lk2)]
    cq1, cq2, ck1, ck2, cv = heads(*ctx_parts)
    k1 = jnp.concatenate([ck1, lk1], axis=2)
    k2 = jnp.concatenate([ck2, lk2], axis=2)
    v = jnp.concatenate([cv, lv], axis=2)
    b, h, t, d = lq1.shape
    nb = t // Q_BLOCK

    def to_blocks(z):
        return z.reshape(b, h, nb, Q_BLOCK, d).transpose(2, 0, 1, 3, 4)

    o_blocks = lax.map(lambda qs: diff_attend(qs[0], qs[1], k1, k2, v, lam), (to_blocks(lq1), to_blocks(lq2)))
    o_lat = o_blocks.transpose(1, 2, 0, 3, 4).reshape(b, h, t, DA_V_DIM)
    out_lat = subln(o_lat)
    out_ctx = subln(diff_attend(cq1, cq2, ck1, ck2, cv, lam)) if with_ctx_out else None
    return out_lat, out_ctx

def peer(h, w_query, sub_keys, u_tab, v_tab):
    b, t, d = h.shape
    blocks = h.reshape(-1, PEER_BLOCK, d)

    def block_fn(xb):
        p = xb.shape[0]
        q = (xb @ w_query).reshape(p, PEER_HEADS, 2, PEER_QDIM // 2)
        s = jnp.einsum('phjd,hjnd->phjn', q, sub_keys).astype(F32)
        sv, si = lax.top_k(s, PEER_TOPK)
        cand = (sv[:, :, 0, :, None] + sv[:, :, 1, None, :]).reshape(p, PEER_HEADS, PEER_TOPK * PEER_TOPK)
        best, ci = lax.top_k(cand, PEER_TOPK)
        i1 = jnp.take_along_axis(si[:, :, 0, :], ci // PEER_TOPK, axis=-1)
        i2 = jnp.take_along_axis(si[:, :, 1, :], ci % PEER_TOPK, axis=-1)
        idx = i1 * PEER_NKEYS + i2
        g = jax.nn.softmax(best, axis=-1)
        act = jax.nn.gelu(jnp.einsum('pd,phkd->phk', xb, u_tab[idx]).astype(F32), approximate=False)
        return jnp.einsum('phk,phkd->pd', (g * act).astype(xb.dtype), v_tab[idx])

    return lax.map(block_fn, blocks).reshape(b, t, d)

def setup_inputs(seed: int = 0) -> dict:
    key = jax.random.key(seed)
    ks = jax.random.split(key, 22)
    L = DEPTH

    def nrm(k, shape, s):
        return jax.random.normal(k, shape, jnp.float32) * s

    return {
        'x': nrm(ks[0], (BATCH, SEQ, D_MODEL), 1.0),
        'c': nrm(ks[1], (BATCH, D_MODEL), 1.0),
        'ctx': nrm(ks[2], (BATCH, CTX_LEN, D_MODEL), 1.0),
        'c_ctx': nrm(ks[3], (D_MODEL,), 1.0),
        'w_ada': nrm(ks[4], (L, D_MODEL, 6 * D_MODEL), 0.5 * D_MODEL ** -0.5),
        'b_ada': nrm(ks[5], (L, 6 * D_MODEL), 0.01),
        'norm1_g': 1.0 + nrm(ks[6], (L, D_MODEL), 0.1),
        'w_in': nrm(ks[7], (L, D_MODEL, IN_COLS), D_MODEL ** -0.5),
        'hg_gamma': nrm(ks[8], (L + 1, 2, HG_WIDTH), 0.5),
        'hg_norm_g': 1.0 + nrm(ks[9], (L, HG_WIDTH), 0.1),
        'da_lambda_q1': nrm(ks[10], (L, DA_HEAD_DIM), 0.1),
        'da_lambda_k1': nrm(ks[11], (L, DA_HEAD_DIM), 0.1),
        'da_lambda_q2': nrm(ks[12], (L, DA_HEAD_DIM), 0.1),
        'da_lambda_k2': nrm(ks[13], (L, DA_HEAD_DIM), 0.1),
        'da_subln_g': 1.0 + nrm(ks[14], (L, DA_WIDTH), 0.1),
        'w_out': nrm(ks[15], (L, MIX_WIDTH, D_MODEL), MIX_WIDTH ** -0.5),
        'norm2_g': 1.0 + nrm(ks[16], (L, D_MODEL), 0.1),
        'peer_w_query': nrm(ks[17], (L, D_MODEL, PEER_HEADS * PEER_QDIM), D_MODEL ** -0.5),
        'peer_sub_keys': nrm(ks[18], (L, PEER_HEADS, 2, PEER_NKEYS, PEER_QDIM // 2), (PEER_QDIM // 2) ** -0.5),
        'peer_u': nrm(ks[19], (L, PEER_EXPERTS, D_MODEL), D_MODEL ** -0.5),
        'peer_v': nrm(ks[20], (L, PEER_EXPERTS, D_MODEL), 0.5),
        'final_norm_g': 1.0 + nrm(ks[21], (D_MODEL,), 0.1),
    }

def reference(x, c, ctx, c_ctx, w_ada, b_ada, norm1_g, w_in, hg_gamma, hg_norm_g,
              da_lambda_q1, da_lambda_k1, da_lambda_q2, da_lambda_k2, da_subln_g, w_out,
              norm2_g, peer_w_query, peer_sub_keys, peer_u, peer_v, final_norm_g):
    n_lat = x.shape[1]
    ROWS = n_lat // GRID_W
    row = jnp.repeat(jnp.arange(ROWS, dtype=F32), GRID_W)
    col = jnp.tile(jnp.arange(GRID_W, dtype=F32), ROWS)
    n_freq = DA_HEAD_DIM // 4
    inv_freq = ROPE_BASE ** (-jnp.arange(n_freq, dtype=F32) / n_freq)
    ang_row = row[:, None] * inv_freq[None, :]
    ang_col = col[:, None] * inv_freq[None, :]
    lb_all = jnp.cumsum(jax.nn.softmax(hg_gamma.astype(F32), axis=0), axis=0)
    c_act = jax.nn.silu(c)[:, None, :]
    cc_act = jax.nn.silu(c_ctx)[None, None, :]
    xc = ctx
    for l in range(DEPTH):
        with_ctx_out = l < DEPTH - 1
        sh1, sc1, g1, sh2, sc2, g2 = jnp.split(c_act @ w_ada[l] + b_ada[l], 6, axis=-1)
        csh1, csc1, cg1, csh2, csc2, cg2 = jnp.split(cc_act @ w_ada[l] + b_ada[l], 6, axis=-1)
        h = rmsnorm(x, norm1_g[l]) * (1.0 + sc1) + sh1
        hc = rmsnorm(xc, norm1_g[l]) * (1.0 + csc1) + csh1
        parts = jnp.split(h @ w_in[l], IN_SPLITS, axis=-1)
        cparts = jnp.split(hc @ w_in[l], IN_SPLITS, axis=-1)
        lam_init = 0.8 - 0.6 * math.exp(-0.3 * l)
        lam = (jnp.exp(jnp.sum(da_lambda_q1[l].astype(F32) * da_lambda_k1[l].astype(F32)))
               - jnp.exp(jnp.sum(da_lambda_q2[l].astype(F32) * da_lambda_k2[l].astype(F32))) + lam_init)
        hg_lat, hg_ctx = hgrn2_mixer(parts[:5], cparts[:5], lb_all[l], hg_norm_g[l], with_ctx_out)
        da_lat, da_ctx = diff_attention(parts[5:], cparts[5:], lam, lam_init, da_subln_g[l],
                                        ang_row, ang_col, with_ctx_out)
        x = x + g1 * (jnp.concatenate([hg_lat, da_lat], axis=-1) @ w_out[l])
        x = x + g2 * peer(rmsnorm(x, norm2_g[l]) * (1.0 + sc2) + sh2,
                          peer_w_query[l], peer_sub_keys[l], peer_u[l], peer_v[l])
        if with_ctx_out:
            xc = xc + cg1 * (jnp.concatenate([hg_ctx, da_ctx], axis=-1) @ w_out[l])
            xc = xc + cg2 * peer(rmsnorm(xc, norm2_g[l]) * (1.0 + csc2) + csh2,
                                 peer_w_query[l], peer_sub_keys[l], peer_u[l], peer_v[l])
    return rmsnorm(x, final_norm_g)


_drawn_inputs = setup_inputs


def setup_inputs(seed=0):
    import zlib

    import numpy as np

    out = dict(_drawn_inputs(seed))
    spreads = {}
    factors = {'b_ada': 3.645,
     'hg_gamma': 6.391,
     'hg_norm_g': 3.222,
     'da_lambda_q1': 8.0,
     'da_lambda_q2': 3.856,
     'da_subln_g': 2.776}
    for name, (base, spread) in spreads.items():
        noise = np.random.default_rng([zlib.crc32(name.encode()), seed]).standard_normal(out[name].shape)
        drawn = base * np.exp(spread * noise) if base else spread * noise
        out[name] = __import__('jax').numpy.asarray(drawn.astype(out[name].dtype))
    for name, factor in factors.items():
        out[name] = (out[name] * factor).astype(out[name].dtype)
    return out
```

```python
import math
from contextlib import ExitStack

import numpy as np
import concourse.bass as bass
from concourse import mybir

F32 = mybir.dt.float32
F32R = mybir.dt.float32r
U8 = mybir.dt.uint8
U32 = mybir.dt.uint32
ALU = mybir.AluOpType
ACT = mybir.ActivationFunctionType
AX = mybir.AxisListType

P = 128
D = 2048
KT = D // P
SEQ = 512
CTX = 256
TOK = CTX + SEQ
HEADS = 8
EPS = 1e-6
ADA1 = 2 * KT
ADA = 6 * KT
UNIT = 4 * 512
TILE = KT * P
LATENT_TILES = 3 * HEADS
IN_TILES = 8 * HEADS
HG_Q, HG_G, DA_Q, HG_FF, HG_FB, HG_I, DA_K, DA_V = range(8)
NT = TOK // P
CT = CTX // P
LT = SEQ // P
LEVELS = 7
PART_OF = (0, 4, 5, 1, 2, 3, 6, 7)
LAM_INIT = 0.8 - 0.6 * math.exp(0.0)
TOPK = 16
NKEYS = 128
E_TILES = NKEYS
PAIR = 2


def adaln_and_norm(nc, k, dram):
    with ExitStack() as ctx:
        sb = lambda n, s, d=F32: ctx.enter_context(nc.sbuf_tensor(n, s, d))
        pb = lambda n: ctx.enter_context(nc.psum_tensor(n, [P, 512], F32))
        sem = lambda n: k.semaphore(nc, n)
        x = sb("x0", [P, KT, TOK])
        xsq = sb("x0_sq", [P, 2, TOK])
        stage = [sb(f"ada_stage{s}", [P, UNIT]) for s in range(4)]
        b_ada = sb("b_ada0", [P, ADA1])
        g1 = sb("norm1_g", [P, KT])
        csig = sb("c_sig", [P, KT, 2])
        craw = sb("c_raw", [P, KT, 2])
        row = sb("ada_row", [2, ADA1 * P])
        mod = sb("mod1", [P, ADA1, 2])
        gain = sb("gain1", [P, KT, 2])
        rstd = sb("rstd1", [P, TOK])
        ss_lat, ss_ctx, p_row, p_col = pb("ss_lat"), pb("ss_ctx"), [pb(f"p_ada_row{s}") for s in range(2)], pb("p_ada_col")
        s_small, s_x, s_c = sem("p0_small_in"), sem("p0_x_in"), sem("p0_ctx_in")
        s_ada = [sem(f"p0_ada_in{s}") for s in range(4)]
        s_sig, s_cact, s_ones = sem("p0_c_sigmoid"), sem("p0_c_act"), sem("p0_ones")
        s_sq, s_sqd, s_ss = sem("p0_squares"), sem("p0_squares_summed"), sem("p0_sums")
        s_adad, s_row, s_col = sem("p0_ada_units_used"), sem("p0_ada_row"), sem("p0_ada_columns")
        s_ln, s_rstd, s_xn, s_mod, s_gain = (sem("p0_ln"), sem("p0_rstd"), sem("p0_x_normed"), sem("p0_mod"),
                                             sem("p0_gain"))
        s_h, s_hi, s_lo = sem("p0_h"), sem("p0_h_hi"), sem("p0_h_lo")
        block = ctx.enter_context(nc.Block())
        chunks = ADA1 * P // 512
        shift_of = lambda t: t // 4 * 8 + t % 4

        @block.sync
        def _(sp):
            sp.dma_start(craw[:], dram["c"]).then_inc(s_small, 16)
            sp.dma_start(b_ada[:], dram["b_ada"][:, 0:ADA1]).then_inc(s_small, 16)
            sp.dma_start(g1[:], dram["norm1_g"]).then_inc(s_small, 16)
            sp.dma_start(k.ident[:], dram["ident"]).then_inc(s_small, 16)
            sp.dma_start(x[:, :, 0:CTX], dram["ctx"]).then_inc(s_c, 16)
            sp.dma_start(x[:, :, CTX:TOK], dram["x"]).then_inc(s_x, 16)
            with sp.Fori(0, chunks) as i:
                for s in range(4):
                    sp.wait_ge(s_adad, 4 * i + s + 1)
                    sp.dma_start(stage[s][:], dram["w_ada"][bass.ds(i, 1), :, s * UNIT:(s + 1) * UNIT].rearrange("a p n -> (a p) n")).then_inc(s_ada[s], 16)

        @block.gpsimd
        def _(pool):
            nc.gpsimd.memset(k.ones[:], 1.0).then_inc(s_ones, 1)
            nc.gpsimd.memset(k.eps[:], EPS).then_inc(s_ones, 1)

        @block.scalar
        def _(act):
            act.wait_ge(s_small, 64)
            nc.scalar.activation(csig[:], craw[:], ACT.Sigmoid).then_inc(s_sig, 1)
            act.wait_ge(s_c, 16)
            act.wait_ge(s_x, 16)
            for t in range(KT):
                if t >= 2:
                    act.wait_ge(s_sqd, t - 1)
                nc.scalar.activation(xsq[:, t % 2, :], x[:, t, :], ACT.Square).then_inc(s_sq, 1)
            act.wait_ge(s_ones, 2)
            act.wait_ge(s_sqd, KT)
            nc.scalar.activation(rstd[:, 0:CTX], ss_ctx[:, 0:CTX], ACT.Ln, bias=k.eps[:], scale=1.0 / D).then_inc(s_ln, 1)
            nc.scalar.activation(rstd[:, CTX:TOK], ss_lat[:], ACT.Ln, bias=k.eps[:], scale=1.0 / D).then_inc(s_ln, 1)
            act.wait_ge(s_ln, 2)
            nc.scalar.activation(rstd[:], rstd[:], ACT.Exp, scale=-0.5).then_inc(s_rstd, 1)
            for t in range(KT):
                act.wait_ge(s_xn, t + 1)
                act.wait_ge(s_gain, t // 4 + 1)
                for j, (a, b) in enumerate(((CTX, TOK), (0, CTX))):
                    nc.scalar.activation(x[:, t, a:b], x[:, t, a:b], ACT.Identity, bias=mod[:, shift_of(t), j:j + 1],
                                         scale=gain[:, t, j:j + 1]).then_inc(s_h, 1)

        @block.vector
        def _(dve):
            dve.sem_inc(s_row, 2)
            dve.wait_ge(s_sig, 1)
            nc.vector.tensor_tensor(k.c_act[:], craw[:], csig[:], ALU.mult).then_inc(s_cact, 1)
            dve.wait_ge(s_rstd, 1)

            def split(t):
                dve.wait_ge(s_h, 2 * t + 2)
                nc.vector.tensor_copy(k.h_hi[:, t, :], x[:, t, :]).then_inc(s_hi, 1)
                dve.wait_ge(s_hi, t + 1)
                nc.vector.tensor_tensor(k.h_lo[:, t, :], x[:, t, :], k.h_hi[:, t, :].bitcast(F32), ALU.subtract).then_inc(s_lo, 1)

            for p in range(chunks // 2):
                quarter = range(4 * p, 4 * p + 4)
                for t in quarter:
                    nc.vector.tensor_tensor(x[:, t, :], x[:, t, :], rstd[:], ALU.mult).then_inc(s_xn, 1)
                for c in range(2 * p, 2 * p + 2):
                    dve.wait_ge(s_adad, 4 * c + 8)
                    nc.vector.tensor_copy(row[:, c * 512:(c + 1) * 512], p_row[c % 2][0:2, :]).then_inc(s_row, 1)
                dve.wait_ge(s_col, p + 1)
                cols = p_col[:, 16 * p:16 * p + 16].rearrange("p (a j) -> p a j", j=2)
                for j in range(2):
                    last = nc.vector.tensor_tensor(mod[:, 8 * p:8 * p + 8, j], cols[:, :, j], b_ada[:, 8 * p:8 * p + 8], ALU.add)
                last.then_inc(s_mod, 1)
                dve.wait_ge(s_mod, p + 1)
                for j in range(2):
                    last = nc.vector.scalar_tensor_tensor(gain[:, 4 * p:4 * p + 4, j], mod[:, 8 * p + 4:8 * p + 8, j], 1.0,
                                                          g1[:, 4 * p:4 * p + 4], ALU.add, ALU.mult)
                last.then_inc(s_gain, 1)
                for t in quarter:
                    split(t)

        @block.tensor
        def _(pe):
            pe.sem_inc(s_adad, 4)
            pe.wait_ge(s_ones, 2)
            for t in range(KT):
                pe.wait_ge(s_sq, t + 1)
                nc.tensor.matmul(ss_ctx[:, 0:CTX], k.ones[:], xsq[:, t % 2, 0:CTX], start=t == 0, stop=t == KT - 1)
                nc.tensor.matmul(ss_lat[:], k.ones[:], xsq[:, t % 2, CTX:TOK], start=t == 0, stop=t == KT - 1).then_inc(s_sqd, 1)
            pe.wait_ge(s_cact, 1)
            for p in range(chunks // 2):
                for c in range(2 * p, 2 * p + 2):
                    pe.wait_ge(s_row, c + 1)
                    for s in range(4):
                        pe.wait_ge(s_ada[s], 16 * c + 16)
                        for t in range(4):
                            last = nc.tensor.matmul(p_row[c % 2][0:2, :], k.c_act[:, 4 * s + t, :], stage[s][:, t * 512:(t + 1) * 512],
                                                    start=s + t == 0, stop=s + t == 6)
                        last.then_inc(s_adad, 1)
                pe.wait_ge(s_row, 2 * p + 4)
                if p >= 1:
                    pe.wait_ge(s_mod, p)
                for t in range(8 * p, 8 * p + 8):
                    last = nc.tensor.matmul(p_col[:, 2 * t:2 * t + 2], row[:, t * P:(t + 1) * P], k.ident[0:2, 0:2],
                                            start=True, stop=True)
                last.then_inc(s_col, 1)


def input_projection(nc, k, dram):
    with ExitStack() as ctx:
        sb = lambda n, s, d=F32: ctx.enter_context(nc.sbuf_tensor(n, s, d))
        pb = lambda n: ctx.enter_context(nc.psum_tensor(n, [P, 512], F32))
        sem = lambda n: k.semaphore(nc, n)
        stage = [sb(f"win_stage{s}", [P, UNIT]) for s in range(2)]
        w_hi = [sb(f"win_hi{s}", [P, UNIT], F32R) for s in range(2)]
        w_lo = [sb(f"win_lo{s}", [P, UNIT], F32R) for s in range(2)]
        ada = [sb(f"ada2_stage{s}", [P, UNIT]) for s in range(2)]
        acc = [sb(f"ada2_acc{s}", [P, 512]) for s in range(2)]
        out = sb("proj_out", [P, 6, 512])
        b_ada = sb("b_ada1", [P, ADA - ADA1])
        p_lat, p_ctx, p_mod = [pb(f"proj_lat{s}") for s in range(4)], [pb(f"proj_ctx{s}") for s in range(2)], pb("p_ada1")
        s_w = [sem(f"p1_w_in{s}") for s in range(2)]
        s_a = [sem(f"p1_ada_in{s}") for s in range(2)]
        s_b = sem("p1_bias_in")
        s_hi, s_lo, s_mm, s_acc, s_modp, s_mod = (sem("p1_w_hi"), sem("p1_w_lo"), sem("p1_units_multiplied"),
                                                  sem("p1_ada_steps"), sem("p1_ada_columns"), sem("p1_mod"))
        s_lat, s_ctx = sem("p1_lat_banks_full"), sem("p1_ctx_banks_full")
        s_evl, s_evc = sem("p1_lat_banks_read"), sem("p1_ctx_banks_read")
        s_st = [sem("p1_lat_stored"), sem("p1_ctx_stored")]
        block = ctx.enter_context(nc.Block())
        groups = IN_TILES // 4
        lat_groups = LATENT_TILES // 4
        loops = ((0, lat_groups, False), (lat_groups, groups, True))
        credit = 5

        def blocks(g, u, context):
            per_unit = 6 if context else 4
            return 4 * per_unit * g + (per_unit * u + credit - (8 * lat_groups if context else 0))


        @block.sync
        def _(sp):
            sp.dma_start(b_ada[:], dram["b_ada"][:, ADA1:ADA]).then_inc(s_b, 16)
            with sp.Fori(0, groups) as g:
                for u in range(4):
                    sp.wait_ge(s_lo, 4 * g + u + 1)
                    sp.dma_start(stage[u % 2][:], dram["w_in"][bass.ds(g, 1), :, u * UNIT:(u + 1) * UNIT].rearrange("a p n -> (a p) n")).then_inc(s_w[u % 2], 16)
                    sp.wait_ge(s_acc, 16 * g + 4 * u + 4)
                    sp.dma_start(ada[u % 2][:], dram["w_ada"][bass.ds(g + ADA1 // 4, 1), :, u * UNIT:(u + 1) * UNIT].rearrange("a p n -> (a p) n")).then_inc(s_a[u % 2], 16)

        @block.scalar
        def _(act):
            act.sem_inc(s_evl, 4)
            act.sem_inc(s_evc, 2)
            act.sem_inc(s_mod, 1)
            act.sem_inc(s_st[0], 64)
            act.sem_inc(s_st[1], 32)
            act.wait_ge(s_b, 16)
            for a, b, context in loops:
                with act.Fori(a // 2, b // 2) as gg:
                    for q in range(2):
                        g = 2 * gg + q
                        for c in range(4):
                            act.wait_ge(s_st[0], 64 * g + 64)
                            act.wait_ge(s_mm, blocks(g, 3, context) + (c + 1))
                            nc.scalar.activation(out[:, c, :], p_lat[c][:], ACT.Copy).then_inc(s_evl, 1)
                            act.wait_ge(s_evl, 4 * g + (c + 5))
                            act.dma_start(dram["proj_lat"][bass.ds(4 * g + c, 1)].rearrange("a p n -> (a p) n"), out[:, c, :]).then_inc(s_st[0], 16)
                        for c in range(2 if context else 0):
                            act.wait_ge(s_st[1], 32 * (g - lat_groups) + 32)
                            act.wait_ge(s_mm, blocks(g, 3, context) + (c + 5))
                            nc.scalar.activation(out[:, 4 + c, :], p_ctx[c][:], ACT.Copy).then_inc(s_evc, 1)
                            act.wait_ge(s_evc, 2 * g + (c + 3 - 2 * lat_groups))
                            act.dma_start(dram["proj_ctx"][bass.ds(gg - lat_groups // 2, 1), c, :, q * 512:(q + 1) * 512].rearrange("a p n -> (a p) n"),
                                          out[:, 4 + c, :]).then_inc(s_st[1], 16)
                        act.wait_ge(s_modp, g + 3)
                        nc.scalar.activation(k.mod2[:, bass.ds(4 * g, 4)], p_mod[:, 0:4], ACT.Copy).then_inc(s_mod, 1)
            act.wait_ge(s_st[0], 64 * groups + 64)
            act.wait_ge(s_st[1], 32 * (groups - lat_groups) + 32)

        @block.vector
        def _(dve):
            dve.sem_inc(s_lo, 2)
            dve.sem_inc(s_acc, 8)
            for a, b, context in loops:
                with dve.Fori(a // 2, b // 2) as gg:
                    for q in range(2):
                        for u in range(4):
                            n, s = 8 * gg + (4 * q + u), u % 2
                            dve.wait_ge(s_w[s], 64 * gg + (32 * q + 16 * (u // 2) + 16))
                            dve.wait_ge(s_mm, blocks(2 * gg + q, u, context) - 4)
                            nc.vector.tensor_copy(w_hi[s][:], stage[s][:]).then_inc(s_hi, 1)
                            dve.wait_ge(s_hi, n + 1)
                            nc.vector.tensor_tensor(w_lo[s][:], stage[s][:], w_hi[s][:].bitcast(F32), ALU.subtract).then_inc(s_lo, 1)
                            dve.wait_ge(s_a[s], 64 * gg + (32 * q + 16 * (u // 2) + 16))
                            for t in range(4):
                                w = ada[s][:, t * 512:(t + 1) * 512]
                                c = k.c_act[:, 4 * u + t, 0:1]
                                dve.wait_ge(s_acc, 4 * n + (t + 8))
                                if u + t == 0:
                                    dve.wait_ge(s_modp, 2 * gg + (q + 1))
                                    nc.vector.tensor_scalar(acc[q][:], w, c, None, ALU.mult).then_inc(s_acc, 1)
                                else:
                                    nc.vector.scalar_tensor_tensor(acc[q][:], w, c, acc[q][:], ALU.mult, ALU.add).then_inc(s_acc, 1)
            dve.wait_ge(s_b, 16)
            dve.wait_ge(s_mod, groups + 1)
            nc.vector.tensor_tensor(k.mod2[:], k.mod2[:], b_ada[:], ALU.add)

        @block.tensor
        def _(pe):
            pe.sem_inc(s_mm, credit)
            pe.sem_inc(s_modp, 2)
            for a, b, context in loops:
                with pe.Fori(a // 2, b // 2) as gg:
                    for q in range(2):
                        g = 2 * gg + q
                        for u in range(4):
                            s = u % 2
                            pe.wait_ge(s_lo, 4 * g + (u + 3))
                            for c in range(4):
                                if u == 0:
                                    pe.wait_ge(s_evl, 4 * g + (c + 1))
                                for t in range(4):
                                    w, kt, h = slice(t * 512 + c * P, t * 512 + (c + 1) * P), 4 * u + t, slice(CTX, TOK)
                                    nc.tensor.matmul(p_lat[c][:], w_hi[s][:, w], k.h_hi[:, kt, h], start=kt == 0, stop=False)
                                    nc.tensor.matmul(p_lat[c][:], w_hi[s][:, w], k.h_lo[:, kt, h], start=False, stop=False)
                                    last = nc.tensor.matmul(p_lat[c][:], w_lo[s][:, w], k.h_hi[:, kt, h], start=False, stop=kt == KT - 1)
                                last.then_inc(s_mm, 1)
                            for c in range(2 if context else 0):
                                if u == 0:
                                    pe.wait_ge(s_evc, 2 * g + (c + 1 - 2 * lat_groups))
                                for t in range(4):
                                    w, kt, h = slice(t * 512, (t + 1) * 512), 4 * u + t, slice(c * P, (c + 1) * P)
                                    nc.tensor.matmul(p_ctx[c][:], k.h_hi[:, kt, h], w_hi[s][:, w], start=kt == 0, stop=False)
                                    nc.tensor.matmul(p_ctx[c][:], k.h_lo[:, kt, h], w_hi[s][:, w], start=False, stop=False)
                                    last = nc.tensor.matmul(p_ctx[c][:], k.h_hi[:, kt, h], w_lo[s][:, w], start=False, stop=kt == KT - 1)
                                last.then_inc(s_mm, 1)
                        pe.wait_ge(s_acc, 16 * g + 24)
                        pe.wait_ge(s_mod, g + 1)
                        for c in range(4):
                            last = nc.tensor.matmul(p_mod[:, c:c + 1], acc[q][:, c * P:(c + 1) * P], k.ones[:, 0:1], start=True, stop=True)
                        last.then_inc(s_modp, 1)


def mixers(nc, k, dram):
    with ExitStack() as ctx:
        sb = lambda n, s, d=F32: ctx.enter_context(nc.sbuf_tensor(n, s, d))
        pb = lambda n, w: ctx.enter_context(nc.psum_tensor(n, [P, w], F32))
        sem = lambda n: k.semaphore(nc, n)
        lat = [sb(f"head_lat{s}", [P, 8, SEQ]) for s in range(2)]
        cx = [sb(f"head_ctx{s}", [P, 5, CT, P]) for s in range(2)]
        perm, cos, sin = sb("rope_perm", [P, P]), sb("rope_cos", [P, SEQ]), sb("rope_sin", [P, SEQ])
        masks = sb("level_masks", [P, LEVELS, P], U8)
        gamma, lamv = sb("gamma", [P, 2, 2, HEADS]), sb("lam_vectors", [P, 4, 64])
        hgn, dan = sb("hg_norm_g", [P, HEADS]), sb("da_subln_g", [P, HEADS])
        lb, omlb, gdiff = sb("lower_bound", [P, 2, HEADS]), sb("one_minus_lb", [P, 2, HEADS]), sb("gamma_diff", [P, 2, HEADS])
        lamp, lams, lame, neglam = sb("lam_prod", [P, 2, 64]), sb("lam_sums", [P, 2]), sb("lam_exp", [P, 2]), sb("neg_lam", [P, 1])
        sq, sg = sb("q_sigmoid", [P, SEQ]), sb("g_sigmoid", [P, SEQ])
        f = [sb(f"forget{d}", [P, TOK]) for d in range(2)]
        key = [sb(f"hg_key{d}", [P, TOK]) for d in range(2)]
        lf = [sb(f"log_forget{d}", [P, TOK]) for d in range(2)]
        cum = [sb(f"cum{d}", [P, NT, P + 1]) for d in range(2)]
        q, gate = sb("hg_query", [P, SEQ]), sb("hg_gate", [P, SEQ])
        kt, qt = sb("da_key", [P, TOK]), sb("da_query", [P, SEQ])
        ropet = sb("rope_tmp", [P, 2, SEQ])
        iv = [sb(f"i_v_tokens{s}", [P, 2, LT, P]) for s in range(2)]
        nmx, nb, sums, rinv, rlam = (sb("neg_max", [P, 8]), sb("exp_bias", [P, 8]), sb("exp_sums", [P, 8]),
                                     sb("exp_inv", [P, 8]), sb("lam_inv", [P, 4]))
        ex = [[sb(f"exp{c}_{s}", [P, TOK]) for s in range(2)] for c in range(2)]
        pt = [sb(f"prob_t{s}", [P, TOK]) for s in range(2)]
        sqd, sqh, rd, rh = sb("da_sq", [P, SEQ]), sb("hg_sq", [P, SEQ]), sb("da_rstd", [P, SEQ]), sb("hg_rstd", [P, SEQ])
        lev = [sb(f"level_operands{s}", [P, 2, SEQ]) for s in range(2)]
        mask_in = lev[0][:].rearrange("p a n -> p (a n)")[:, 0:LEVELS * P].rearrange("p (l n) -> p l n", n=P)
        diag, sc = sb("diag_key", [P, SEQ]), sb("intra_scores", [P, SEQ])
        kd = [sb(f"key_decayed{d}", [P, NT, P]) for d in range(2)]
        kdt = [sb(f"key_decayed_t{d}", [P, NT, P]) for d in range(2)]
        qi = [sb(f"query_decayed{d}", [P, LT, P]) for d in range(2)]
        dc = [sb(f"chunk_decay{d}", [P, NT]) for d in range(2)]
        st = [sb(f"states{d}", [P, 5, P]) for d in range(2)]
        hgo = sb("hg_out", [P, SEQ])
        A, B, C, E, F = pb("bank_a", 1024), pb("bank_b", 1024), pb("bank_c", 1024), pb("bank_e", 512), pb("bank_f", 512)

        names = ("const_in lam_steps ready done tctx sig tctx_read rot tlat tlat_read cos f_steps f key lf scan cum q gate "
                 "rope_tmp kq s mx nb e inv p_scaled p tp tp_read pv dsq dss dln drs diag x ex ab lv sc kda qia kde kd qie qi "
                 "turn tkd tkd_read dc u state o hsq hss hln hrs hmul")
        z = {n: sem("p2_" + n) for n in names.split()}
        s_in = [sem(f"p2_in{s}") for s in range(2)]
        block = ctx.enter_context(nc.Block())

        CREDITS = {"lv": 1, "o": 1, "s": 8, "gate": 1, "hmul": 1, "hln": 1}

        def heads(eng):
            with eng.Fori(0, HEADS // 2 - 1) as hh:
                for par in range(2):
                    yield hh, 2 * hh + par, par, (hh + (1 if par else 0), 2 * hh + (par + 1), 1 - par)
            for h in (HEADS - 2, HEADS - 1):
                yield h // 2, h, h % 2, ((h + 1) // 2, h + 1, (h + 1) % 2) if h + 1 < HEADS else None

        def W(eng, name, per_head, h, n):
            eng.wait_ge(z[name], per_head * h + (n + CREDITS.get(name, 0)))

        def half(ap, L, second):
            v = ap.rearrange("p (b s j) -> p b s j", s=2, j=L)
            return v[:, :, second, :]

        def cumv(c, L, off, n):
            nb_ = P // (2 * L)
            base = cum[c][:, CT:NT, off:off + 1]
            v = cum[c][:, CT:NT, :]
            if off + P <= P + 1:
                v = cum[c][:, CT:NT, off:off + P].rearrange("p t (b r) -> p t b r", r=2 * L)
                return v[:, :, :, 0:n]
            v = cum[c][:, CT:NT, off - L:off - L + P].rearrange("p t (b r) -> p t b r", r=2 * L)
            return v[:, :, :, L:L + n]

        def halfv(ap, L, second):
            return ap.rearrange("p (t b s j) -> p t b s j", t=LT, s=2, j=L)[:, :, :, second, :]

        @block.sync
        def _(sp):
            for dst, name in ((perm, "rope_perm"), (cos, "rope_cos"), (sin, "rope_sin"),
                              (gamma, "hg_gamma"), (hgn, "hg_norm_g"), (dan, "da_subln_g")):
                sp.dma_start(dst[:], dram[name]).then_inc(z["const_in"], 16)
            sp.dma_start(mask_in, dram["level_masks"]).then_inc(z["const_in"], 16)
            sp.dma_start(lamv[:], dram["da_lambda"].to_broadcast([P, 4, 64])).then_inc(z["const_in"], 16)
            pl = dram["proj_lat"].rearrange("(a h) p n -> h p a n", a=8)
            pc = dram["proj_ctx"]
            for hh, h, par, _ in heads(sp):
                W(sp, "done", 1, h, 1)
                sp.dma_start(lat[par][:], pl[bass.ds(h, 1)].rearrange("o p a n -> (o p) a n")).then_inc(s_in[par], 16)
                for a in range(5):
                    sp.dma_start(cx[par][:, a], pc[a, :, :, bass.ds(P * h, P)].rearrange("c p n -> p c n")).then_inc(s_in[par], 16)

        IN = 96

        @block.gpsimd
        def _(pool):
            pool.wait_ge(z["const_in"], 128)

            def prologue(hh, h, par):
                pool.wait_ge(s_in[par], IN * hh + IN)
                W(pool, "s", 8, h, 0)
                nc.gpsimd.tensor_tensor(kt[:, CTX:TOK], lat[par][:, DA_K], cos[:], ALU.mult).then_inc(z["cos"], 1)
                nc.gpsimd.tensor_tensor(qt[:], lat[par][:, DA_Q], cos[:], ALU.mult).then_inc(z["cos"], 1)

            prologue(0, 0, 0)
            for hh, h, par, after in heads(pool):
                W(pool, "cum", 2, h, 2)
                for l in range(LEVELS):
                    L = P >> (l + 1)
                    nb_ = P // (2 * L)
                    W(pool, "lv", 8, h, l)
                    o = lev[l % 2]
                    ref = [cumv(c, L, L, 1).to_broadcast([P, LT, nb_, L]) for c in range(2)]
                    nc.gpsimd.tensor_tensor(halfv(o[:, 0], L, 0), ref[0], cumv(0, L, 1, L), ALU.subtract)
                    nc.gpsimd.tensor_tensor(halfv(o[:, 0], L, 1), cumv(1, L, L, L), ref[1], ALU.subtract)
                    nc.gpsimd.tensor_tensor(halfv(o[:, 1], L, 0), ref[1], cumv(1, L, 0, L), ALU.subtract)
                    nc.gpsimd.tensor_tensor(halfv(o[:, 1], L, 1), cumv(0, L, L + 1, L), ref[0], ALU.subtract).then_inc(z["x"], 1)
                    if l == 1:
                        W(pool, "o", 1, h, 0)
                        nc.gpsimd.tensor_tensor(kd[0][:], cum[0][:, :, P:P + 1].to_broadcast([P, NT, P]), cum[0][:, :, 1:P + 1], ALU.subtract).then_inc(z["kda"], 1)
                        nc.gpsimd.tensor_tensor(qi[1][:], cum[1][:, CT:NT, P:P + 1].to_broadcast([P, LT, P]), cum[1][:, CT:NT, 0:P], ALU.subtract).then_inc(z["qia"], 1)
                if after:
                    prologue(*after)

        @block.scalar
        def _(act):
            act.wait_ge(z["lam_steps"], 1)
            nc.scalar.activation(lb[:], gdiff[:], ACT.Sigmoid).then_inc(z["lam_steps"], 1)
            act.wait_ge(z["lam_steps"], 4)
            nc.scalar.activation(lame[:], lams[:], ACT.Exp).then_inc(z["lam_steps"], 1)

            def gates(hh, h, par):
                act.wait_ge(s_in[par], IN * hh + IN)
                W(act, "gate", 1, h, 0)
                nc.scalar.activation(sq[:], lat[par][:, HG_Q], ACT.Sigmoid).then_inc(z["sig"], 1)
                nc.scalar.activation(sg[:], lat[par][:, HG_G], ACT.Sigmoid).then_inc(z["sig"], 1)
                for d in range(2):
                    nc.scalar.activation(f[d][:, CTX:TOK], lat[par][:, HG_FF + d], ACT.Sigmoid).then_inc(z["sig"], 1)
                W(act, "tctx", 1, h, 1)
                for d in range(2):
                    nc.scalar.activation(f[d][:, 0:CTX], C[:, d * CTX:(d + 1) * CTX], ACT.Sigmoid).then_inc(z["sig"], 1)
                nc.scalar.activation(kt[:, 0:CTX], C[:, 2 * CTX:3 * CTX], ACT.Copy).then_inc(z["tctx_read"], 1)

            def tokens(hh, h, par):
                W(act, "tlat", 1, h, 1)
                nc.scalar.activation(iv[par][:], C[:].rearrange("p (a t n) -> p a t n", a=2, n=P), ACT.Copy).then_inc(z["tlat_read"], 1)

            def logs(hh, h, par):
                for d in range(2):
                    W(act, "f", 2, h, d + 1)
                    nc.scalar.activation(lf[d][:], f[d][:], ACT.Ln).then_inc(z["lf"], 1)

            gates(0, 0, 0)
            tokens(0, 0, 0)
            logs(0, 0, 0)
            for hh, h, par, after in heads(act):
                def exps(b):
                    for c, bank in enumerate((A, B)):
                        W(act, "nb", 8, h, 2 * b + c + 1)
                        if b >= 2:
                            W(act, "tp", 4, h, b - 1)
                        nc.scalar.activation(ex[c][b % 2][:], bank[:, 0:TOK], ACT.Exp, bias=nb[:, 2 * b + c:2 * b + c + 1],
                                             scale=0.125, accum_out=sums[:, 2 * b + c:2 * b + c + 1]).then_inc(z["e"], 1)

                def prob_t(b):
                    W(act, "tp", 4, h, b + 1)
                    if b >= 2:
                        W(act, "pv", 4, h, b - 1)
                    nc.scalar.activation(pt[b % 2][:], C[:, 0:TOK], ACT.Copy).then_inc(z["tp_read"], 1)

                def level(l):
                    W(act, "x", 7, h, l + 1)
                    nc.scalar.activation(lev[l % 2][:], lev[l % 2][:], ACT.Exp).then_inc(z["ex"], 1)

                exps(0)
                level(0)
                exps(1)
                level(1)
                prob_t(0)
                W(act, "cum", 2, h, 2)
                nc.scalar.activation(qi[0][:], cum[0][:, CT:NT, 1:P + 1], ACT.Exp).then_inc(z["qie"], 1)
                nc.scalar.activation(kd[1][:], cum[1][:, :, 0:P], ACT.Exp).then_inc(z["kde"], 1)
                for d in range(2):
                    nc.scalar.activation(dc[d][:], cum[d][:, :, P], ACT.Exp).then_inc(z["dc"], 1)
                exps(2)
                level(2)
                W(act, "qia", 1, h, 1)
                nc.scalar.activation(qi[1][:], qi[1][:], ACT.Exp).then_inc(z["qie"], 1)
                W(act, "kda", 1, h, 1)
                nc.scalar.activation(kd[0][:], kd[0][:], ACT.Exp).then_inc(z["kde"], 1)
                prob_t(1)
                level(3)
                exps(3)
                level(4)
                prob_t(2)
                level(5)
                prob_t(3)
                level(6)
                W(act, "pv", 4, h, 4)
                nc.scalar.activation(sqd[:], E[:], ACT.Square).then_inc(z["dsq"], 1)
                for d in range(2):
                    W(act, "tkd", 2, h, d + 1)
                    nc.scalar.activation(kdt[d][:], C[:, 0:TOK].rearrange("p (t n) -> p t n", n=P), ACT.Copy).then_inc(z["tkd_read"], 1)
                if after:
                    gates(*after)
                    tokens(*after)
                W(act, "o", 1, h, 1)
                nc.scalar.activation(sqh[:], F[:], ACT.Square).then_inc(z["hsq"], 1)
                W(act, "dss", 1, h, 1)
                nc.scalar.activation(rd[:], A[:, 0:SEQ], ACT.Ln, bias=k.eps[:], scale=1.0 / P).then_inc(z["dln"], 1)
                if after:
                    logs(*after)
                W(act, "hss", 1, h, 1)
                nc.scalar.activation(rh[:], B[:, 0:SEQ], ACT.Ln, bias=k.eps[:], scale=1.0 / P).then_inc(z["hln"], 1)
                W(act, "dln", 1, h, 1)
                nc.scalar.activation(rd[:], rd[:], ACT.Exp, scale=-0.5).then_inc(z["drs"], 1)
                W(act, "hln", 1, h, 1)
                nc.scalar.activation(rh[:], rh[:], ACT.Exp, scale=-0.5).then_inc(z["hrs"], 1)

        @block.vector
        def _(dve):
            v = nc.vector
            dve.sem_inc(z["done"], 2)
            dve.sem_inc(z["gate"], 1)
            dve.sem_inc(z["hmul"], 1)
            dve.wait_ge(z["const_in"], 128)
            v.tensor_copy(masks[:], mask_in)
            v.memset(cum[0][:, :, 0:1], 0.0)
            v.memset(cum[1][:, :, 0:1], 0.0)
            v.tensor_tensor(gdiff[:], gamma[:, 0], gamma[:, 1], ALU.subtract).then_inc(z["lam_steps"], 1)
            v.tensor_tensor(lamp[:], lamv[:, 0:2], lamv[:, 2:4], ALU.mult).then_inc(z["ready"], 1)
            dve.wait_ge(z["lam_steps"], 2)
            v.tensor_scalar(omlb[:], lb[:], -1.0, 1.0, ALU.mult, ALU.add).then_inc(z["lam_steps"], 1)
            dve.wait_ge(z["ready"], 1)
            v.tensor_reduce(lams[:], lamp[:], AX.X, ALU.add).then_inc(z["lam_steps"], 1)
            dve.wait_ge(z["lam_steps"], 5)
            v.tensor_tensor(neglam[:], lame[:, 1:2], lame[:, 0:1], ALU.subtract).then_inc(z["lam_steps"], 1)
            dve.wait_ge(z["lam_steps"], 6)
            v.tensor_scalar(neglam[:], neglam[:], -LAM_INIT, None, ALU.add).then_inc(z["lam_steps"], 1)
            v.tensor_scalar(dan[:], dan[:], 1.0 - LAM_INIT, None, ALU.mult).then_inc(z["lam_steps"], 1)
            dve.wait_ge(z["lam_steps"], 8)

            def forget(hh, h, par):
                W(dve, "sig", 6, h, 1)
                v.tensor_tensor(q[:], lat[par][:, HG_Q], sq[:], ALU.mult).then_inc(z["q"], 1)
                W(dve, "sig", 6, h, 6)
                for d in range(2):
                    col = bass.ds(h, 1)
                    v.tensor_scalar(f[d][:], f[d][:], omlb[:, d, col], lb[:, d, col], ALU.mult, ALU.add).then_inc(z["f_steps"], 1)
                    W(dve, "f_steps", 2, h, d + 1)
                    v.tensor_scalar(key[d][:], f[d][:], -1.0, 1.0, ALU.mult, ALU.add).then_inc(z["key"], 1)
                    W(dve, "key", 2, h, d + 1)
                    v.tensor_scalar(f[d][:], f[d][:], 2.0 ** -63, None, ALU.max).then_inc(z["f"], 1)

            def rotate_and_scan(hh, h, par):
                W(dve, "rot", 2, h, 2)
                v.tensor_tensor(ropet[:], C[:].rearrange("p (j n) -> p j n", j=2), sin[:].rearrange("p (o n) -> p o n", o=1).to_broadcast([P, 2, SEQ]),
                                ALU.mult).then_inc(z["rope_tmp"], 1)
                W(dve, "cos", 2, h, 2)
                W(dve, "rope_tmp", 1, h, 1)
                v.tensor_tensor(kt[:, CTX:TOK], kt[:, CTX:TOK], ropet[:, 0], ALU.add)
                v.tensor_tensor(qt[:], qt[:], ropet[:, 1], ALU.add).then_inc(z["kq"], 1)
                v.tensor_tensor(diag[:], key[0][:, CTX:TOK], key[1][:, CTX:TOK], ALU.add).then_inc(z["diag"], 1)
                for d in range(2):
                    W(dve, "lf", 2, h, d + 1)
                    for t in range(NT):
                        last = v.tensor_tensor_scan(cum[d][:, t, 1:P + 1], k.ones[:], lf[d][:, t * P:(t + 1) * P], 0.0, ALU.mult, ALU.add)
                    last.then_inc(z["cum"], 1)

            forget(0, 0, 0)
            rotate_and_scan(0, 0, 0)
            for hh, h, par, after in heads(dve):
                def maxima(b):
                    for c, bank in enumerate((A, B)):
                        col = slice(2 * b + c, 2 * b + c + 1)
                        W(dve, "s", 8, h, 2 * b + c + 1)
                        v.tensor_reduce(nmx[:, col], bank[:, 0:TOK], AX.X, ALU.max, negate=True).then_inc(z["mx"], 1)
                        W(dve, "mx", 8, h, 2 * b + c + 1)
                        v.tensor_scalar(nb[:, col], nmx[:, col], 0.125, None, ALU.mult).then_inc(z["nb"], 1)

                def probs(b):
                    W(dve, "e", 8, h, 2 * b + 2)
                    v.reciprocal(rinv[:, 2 * b:2 * b + 2], sums[:, 2 * b:2 * b + 2]).then_inc(z["inv"], 1)
                    W(dve, "inv", 8, h, 2 * b + 1)
                    v.tensor_tensor(rlam[:, b:b + 1], rinv[:, 2 * b + 1:2 * b + 2], neglam[:], ALU.mult).then_inc(z["inv"], 1)
                    W(dve, "inv", 8, h, 2 * b + 2)
                    v.tensor_scalar(ex[1][b % 2][:], ex[1][b % 2][:], rlam[:, b:b + 1], None, ALU.mult).then_inc(z["p_scaled"], 1)
                    W(dve, "p_scaled", 4, h, b + 1)
                    v.scalar_tensor_tensor(ex[0][b % 2][:], ex[0][b % 2][:], rinv[:, 2 * b:2 * b + 1], ex[1][b % 2][:], ALU.mult, ALU.add).then_inc(z["p"], 1)

                def operands(l):
                    L = P >> (l + 1)
                    o = lev[l % 2]
                    W(dve, "ex", 7, h, l + 1)
                    for j in range(2):
                        v.tensor_tensor(halfv(o[:, 0], L, j), halfv(o[:, 0], L, j), halfv(key[j][:, CTX:TOK], L, j), ALU.mult)
                    v.tensor_tensor(o[:, 1], o[:, 1], q[:], ALU.mult).then_inc(z["ab"], 1)

                def collect(l):
                    W(dve, "lv", 8, h, l + 1)
                    if l == 0:
                        v.tensor_copy(sc[:], F[:]).then_inc(z["sc"], 1)
                    else:
                        W(dve, "sc", 8, h, l)
                        dve.sem_inc(z["turn"], 1)
                        v.copy_predicated(sc[:].rearrange("p (t n) -> p t n", t=LT), masks[:, l - 1:l].to_broadcast([P, LT, P]),
                                          F[:].rearrange("p (t n) -> p t n", t=LT)).then_inc(z["sc"], 1)

                maxima(0)
                collect(0)
                maxima(1)
                operands(0)
                probs(0)
                collect(1)
                operands(1)
                probs(1)
                maxima(2)
                collect(2)
                operands(2)
                probs(2)
                maxima(3)
                W(dve, "qie", 2, h, 2)
                for d in range(2):
                    last = v.tensor_tensor(qi[d][:], qi[d][:], q[:].rearrange("p (t n) -> p t n", t=LT), ALU.mult)
                last.then_inc(z["qi"], 1)
                W(dve, "kde", 2, h, 2)
                for d in range(2):
                    v.tensor_tensor(kd[d][:], kd[d][:], key[d][:].rearrange("p (t n) -> p t n", t=NT), ALU.mult).then_inc(z["kd"], 1)
                collect(3)
                operands(3)
                probs(3)
                collect(4)
                operands(4)
                collect(5)
                operands(5)
                collect(6)
                operands(6)
                collect(7)
                v.scalar_tensor_tensor(gate[:], lat[par][:, HG_G], hgn[:, bass.ds(h, 1)], sg[:], ALU.mult, ALU.mult).then_inc(z["gate"], 1)
                W(dve, "u", 1, h, 1)
                W(dve, "dc", 2, h, 2)
                uf = [B[:, t * P:(t + 1) * P] for t in range(4)] + [A[:, 512:512 + P]]
                ub = [B[:, 512 + t * P:512 + (t + 1) * P] for t in range(4)] + [A[:, 512 + P:512 + 2 * P]]
                for j in range(5):
                    for d, u, t in ((0, uf[j], j), (1, ub[j], (1, 0, 5, 4, 3)[j])):
                        if j == 0:
                            last = v.tensor_copy(st[d][:, 0], u)
                        else:
                            last = v.scalar_tensor_tensor(st[d][:, j], st[d][:, j - 1], dc[d][:, t:t + 1], u, ALU.mult, ALU.add)
                    last.then_inc(z["state"], 1)
                    if j < 4:
                        W(dve, "state", 5, h, j + 1)
                if after:
                    forget(*after)
                    rotate_and_scan(*after)
                W(dve, "drs", 1, h, 1)
                v.scalar_tensor_tensor(k.mix[:, bass.ds(h + HEADS, 1)].rearrange("p a n -> p (a n)"), E[:], dan[:, bass.ds(h, 1)], rd[:], ALU.mult, ALU.mult).then_inc(z["hmul"], 1)
                W(dve, "hrs", 1, h, 1)
                v.tensor_tensor(hgo[:], F[:], rh[:], ALU.mult).then_inc(z["hmul"], 1)
                W(dve, "hmul", 2, h, 2)
                W(dve, "gate", 1, h, 1)
                v.tensor_tensor(k.mix[:, bass.ds(h, 1)].rearrange("p a n -> p (a n)"), hgo[:], gate[:], ALU.mult).then_inc(z["done"], 1)

        @block.tensor
        def _(pe):
            mm, tr = nc.tensor.matmul, nc.tensor.transpose
            pe.wait_ge(z["const_in"], 128)
            pe.sem_inc(z["lv"], 1)
            pe.sem_inc(z["o"], 1)
            pe.sem_inc(z["hln"], 1)
            pe.sem_inc(z["s"], 8)

            def context_transposed(hh, h, par):
                pe.wait_ge(s_in[par], IN * hh + IN)
                for j, part in enumerate((0, 1, 3)):
                    for t in range(CT):
                        last = tr(C[:, (j * CT + t) * P:(j * CT + t + 1) * P], cx[par][:, part, t], k.ident[:])
                last.then_inc(z["tctx"], 1)

            def latents_rotated(hh, h, par):
                W(pe, "tlat_read", 1, h, 1)
                mm(C[:, 0:SEQ], perm[:], lat[par][:, DA_K], start=True, stop=True).then_inc(z["rot"], 1)
                mm(C[:, SEQ:2 * SEQ], perm[:], lat[par][:, DA_Q], start=True, stop=True).then_inc(z["rot"], 1)

            def latents_transposed(hh, h, par):
                W(pe, "tctx_read", 1, h, 1)
                for j, part in enumerate((HG_I, DA_V)):
                    for t in range(LT):
                        last = tr(C[:, (j * LT + t) * P:(j * LT + t + 1) * P], lat[par][:, part, t * P:(t + 1) * P], k.ident[:])
                last.then_inc(z["tlat"], 1)

            context_transposed(0, 0, 0)
            latents_transposed(0, 0, 0)
            latents_rotated(0, 0, 0)
            for hh, h, par, after in heads(pe):
                def scores(b):
                    for c, bank in enumerate((A, B)):
                        if b >= 1:
                            W(pe, "e", 8, h, 2 * b + c - 1)
                        lanes = slice(64 * c, 64 * c + 64)
                        for lo, hi in ((0, 512), (512, TOK)):
                            last = mm(bank[:, lo:hi], qt[lanes, b * P:(b + 1) * P], kt[lanes, lo:hi], start=True, stop=True)
                        last.then_inc(z["s"], 1)

                def transpose_probs(b):
                    W(pe, "p", 4, h, b + 1)
                    if b == 0:
                        W(pe, "rope_tmp", 1, h, 1)
                    else:
                        W(pe, "tp_read", 4, h, b)
                    for t in range(NT):
                        last = tr(C[:, t * P:(t + 1) * P], ex[0][b % 2][:, t * P:(t + 1) * P], k.ident[:])
                    last.then_inc(z["tp"], 1)

                def attend(b):
                    W(pe, "tp_read", 4, h, b + 1)
                    for t in range(NT):
                        vt = cx[par][:, 4, t] if t < CT else iv[par][:, 1, t - CT]
                        last = mm(E[:, b * P:(b + 1) * P], vt, pt[b % 2][:, t * P:(t + 1) * P], start=t == 0, stop=t == NT - 1)
                    last.then_inc(z["pv"], 1)

                def level(l):
                    if l == 0:
                        W(pe, "diag", 1, h, 1)
                        W(pe, "q", 1, h, 1)
                        W(pe, "hmul", 2, h, 0)
                    else:
                        W(pe, "ab", 7, h, l)
                        W(pe, "sc", 8, h, l)
                    for t in range(LT):
                        w = slice(t * P, (t + 1) * P)
                        a, b_ = (diag[:, w], q[:, w]) if l == 0 else (lev[(l - 1) % 2][:, 0, w], lev[(l - 1) % 2][:, 1, w])
                        last = mm(F[:, w], a, b_, start=True, stop=True)
                    last.then_inc(z["lv"], 1)

                W(pe, "kq", 1, h, 1)
                W(pe, "tctx_read", 1, h, 1)
                W(pe, "hln", 1, h, 0)
                scores(0)
                level(0)
                scores(1)
                level(1)
                transpose_probs(0)
                scores(2)
                level(2)
                attend(0)
                transpose_probs(1)
                scores(3)
                level(3)
                attend(1)
                transpose_probs(2)
                level(4)
                attend(2)
                transpose_probs(3)
                level(5)
                attend(3)
                level(6)
                for d in range(2):
                    W(pe, "kd", 2, h, d + 1)
                    if d == 0:
                        W(pe, "tp_read", 4, h, 4)
                    else:
                        W(pe, "tkd_read", 2, h, 1)
                    for t in range(NT):
                        last = tr(C[:, t * P:(t + 1) * P], kd[d][:, t], k.ident[:])
                    last.then_inc(z["tkd"], 1)
                W(pe, "dsq", 1, h, 1)
                W(pe, "e", 8, h, 8)
                mm(A[:, 0:SEQ], k.ones[:], sqd[:], start=True, stop=True).then_inc(z["dss"], 1)
                level(7)
                W(pe, "tkd_read", 2, h, 2)
                if after:
                    context_transposed(*after)
                for j in range(5):
                    for d, t in ((0, j), (1, (1, 0, 5, 4, 3)[j])):
                        vt = cx[par][:, 2, t] if t < CT else iv[par][:, 0, t - CT]
                        out = B[:, d * 512 + j * P:d * 512 + (j + 1) * P] if j < 4 else A[:, 512 + d * P:512 + (d + 1) * P]
                        last = mm(out, kdt[d][:, t], vt, start=True, stop=True)
                last.then_inc(z["u"], 1)
                if after:
                    latents_transposed(*after)
                W(pe, "sc", 8, h, 8)
                W(pe, "qi", 1, h, 1)
                W(pe, "state", 5, h, 5)
                for t in range(LT):
                    w = slice(t * P, (t + 1) * P)
                    mm(F[:, w], iv[par][:, 0, t], sc[:, w], start=True, stop=False)
                    mm(F[:, w], st[0][:, t + 1], qi[0][:, t], start=False, stop=False)
                    last = mm(F[:, w], st[1][:, LT - t], qi[1][:, t], start=False, stop=True)
                last.then_inc(z["o"], 1)
                if after:
                    latents_rotated(*after)
                W(pe, "hsq", 1, h, 1)
                mm(B[:, 0:SEQ], k.ones[:], sqh[:], start=True, stop=True).then_inc(z["hss"], 1)


def output_and_query(nc, k, dram):
    with ExitStack() as ctx:
        sb = lambda n, s, d=F32: ctx.enter_context(nc.sbuf_tensor(n, s, d))
        pb = lambda n: ctx.enter_context(nc.psum_tensor(n, [P, 512], F32))
        sem = lambda n: k.semaphore(nc, n)
        stage = [sb(f"wo_stage{s}", [P, UNIT]) for s in range(2)]
        w_hi = [sb(f"wo_hi{s}", [P, UNIT // 2], F32R) for s in range(2)]
        w_lo = [sb(f"wo_lo{s}", [P, UNIT // 2], F32R) for s in range(2)]
        g2n, gain = sb("norm2_g", [P, KT]), sb("gain2", [P, KT])
        tmp = sb("x_delta", [P, 2, SEQ])
        xsq = sb("x1_sq", [P, 2, SEQ])
        rstd = sb("rstd2", [P, SEQ])
        p_out, p_ss = [pb(f"wo_out{s}") for s in range(4)], pb("ss2")
        names = "in mix_hi mix_lo hi lo mm ev x1 sq sqd ln rstd gain xn h h_hi h_lo qev"
        z = {n: sem("p3_" + n) for n in names.split()}
        s_w = [sem(f"p3_w_in{s}") for s in range(2)]
        block = ctx.enter_context(nc.Block())
        G = D // 512
        HALF = UNIT // 2

        @block.sync
        def _(sp):
            sp.dma_start(k.x[:], dram["x"]).then_inc(z["in"], 16)
            sp.dma_start(g2n[:], dram["norm2_g"]).then_inc(z["in"], 16)
            for w_name, first in (("w_out", 0), ("w_query", G)):
                with sp.Fori(0, G) as g:
                    for u in range(4):
                        sp.wait_ge(z["lo"], 8 * g + (8 * first + 2 * u + 1))
                        sp.dma_start(stage[u % 2][:], dram[w_name][bass.ds(g, 1), :, u * UNIT:(u + 1) * UNIT].rearrange("a p n -> (a p) n")).then_inc(s_w[u % 2], 16)

        @block.gpsimd
        def _(pool):
            pool.wait_ge(z["in"], 32)
            with pool.Fori(0, G) as g:
                for c in range(4):
                    tile = bass.ds(4 * g + c, 1)
                    pool.wait_ge(z["ev"], 4 * g + c + 5)
                    nc.gpsimd.tensor_tensor(k.x[:, tile].rearrange("p a n -> p (a n)"), k.x[:, tile].rearrange("p a n -> p (a n)"),
                                            tmp[:, c % 2], ALU.add).then_inc(z["x1"], 1)

        @block.scalar
        def _(act):
            act.sem_inc(z["ev"], 4)
            act.wait_ge(z["in"], 32)
            with act.Fori(0, G) as g:
                for c in range(4):
                    act.wait_ge(z["mm"], 32 * g + (28 + c + 1 + 8))
                    act.wait_ge(z["x1"], 4 * g + c + 1)
                    nc.scalar.activation(tmp[:, c % 2], p_out[c][:], ACT.Copy, scale=k.mod2[:, bass.ds(4 * g + c, 1)]).then_inc(z["ev"], 1)
                for c in range(4):
                    act.wait_ge(z["x1"], 4 * g + c + 3)
                    act.wait_ge(z["sqd"], 4 * g + c + 1)
                    nc.scalar.activation(xsq[:, c % 2], k.x[:, bass.ds(4 * g + c, 1)].rearrange("p a n -> p (a n)"), ACT.Square).then_inc(z["sq"], 1)
            act.wait_ge(z["sqd"], KT + 2)
            nc.scalar.activation(rstd[:], p_ss[:], ACT.Ln, bias=k.eps[:], scale=1.0 / D).then_inc(z["ln"], 1)
            act.wait_ge(z["ln"], 1)
            nc.scalar.activation(rstd[:], rstd[:], ACT.Exp, scale=-0.5).then_inc(z["rstd"], 1)
            act.wait_ge(z["gain"], 1)
            for t in range(KT):
                act.wait_ge(z["xn"], t + 1)
                nc.scalar.activation(k.q[:, t], k.q[:, t], ACT.Identity, bias=k.mod2[:, KT + t:KT + t + 1], scale=gain[:, t:t + 1]).then_inc(z["h"], 1)
            with act.Fori(G, 2 * G) as g:
                for c in range(4):
                    act.wait_ge(z["mm"], 32 * g + (28 + c + 1 + 8))
                    act.wait_ge(z["h_lo"], KT)
                    nc.scalar.activation(k.q[:, bass.ds(4 * g + (c - 4 * G), 1)].rearrange("p a n -> p (a n)"), p_out[c][:], ACT.Copy).then_inc(z["ev"], 1)

        @block.vector
        def _(dve):
            v = nc.vector
            dve.sem_inc(z["lo"], 3)

            def split(g, u, j, first):
                n = 8 * first + 2 * u + j
                dve.wait_ge(s_w[u % 2], 32 * g + (32 * first + 16 * (u // 2) + 16))
                dve.wait_ge(z["mm"], 32 * g + (4 * n + 4))
                w = slice(j * HALF, (j + 1) * HALF)
                v.tensor_copy(w_hi[j][:], stage[u % 2][:, w]).then_inc(z["hi"], 1)
                dve.wait_ge(z["hi"], 8 * g + (n + 1))
                v.tensor_tensor(w_lo[j][:], stage[u % 2][:, w], w_hi[j][:].bitcast(F32), ALU.subtract).then_inc(z["lo"], 1)

            for t in range(KT):
                v.tensor_copy(k.a_hi[:, t], k.mix[:, t]).then_inc(z["mix_hi"], 1)
                dve.wait_ge(z["mix_hi"], t + 1)
                v.tensor_tensor(k.a_lo[:, t], k.mix[:, t], k.a_hi[:, t].bitcast(F32), ALU.subtract).then_inc(z["mix_lo"], 1)
                if t == 0:
                    split(0, 0, 0, 0)
                    split(0, 0, 1, 0)
            for u in range(1, 4):
                for j in range(2):
                    split(0, u, j, 0)
            with dve.Fori(1, G) as g:
                for u in range(4):
                    for j in range(2):
                        split(g, u, j, 0)
            for j in range(2):
                split(0, 0, j, G)
            dve.wait_ge(z["in"], 32)
            v.scalar_tensor_tensor(gain[:], k.mod2[:, 2 * KT:3 * KT], 1.0, g2n[:], ALU.add, ALU.mult).then_inc(z["gain"], 1)
            dve.wait_ge(z["rstd"], 1)
            for t in range(KT):
                v.tensor_tensor(k.q[:, t], k.x[:, t], rstd[:], ALU.mult).then_inc(z["xn"], 1)
                if t >= 1:
                    dve.wait_ge(z["h"], t)
                    v.tensor_copy(k.a_hi[:, t - 1], k.q[:, t - 1]).then_inc(z["h_hi"], 1)
                    dve.wait_ge(z["h_hi"], t)
                    v.tensor_tensor(k.a_lo[:, t - 1], k.q[:, t - 1], k.a_hi[:, t - 1].bitcast(F32), ALU.subtract).then_inc(z["h_lo"], 1)
            dve.wait_ge(z["h"], KT)
            v.tensor_copy(k.a_hi[:, KT - 1], k.q[:, KT - 1]).then_inc(z["h_hi"], 1)
            dve.wait_ge(z["h_hi"], KT)
            v.tensor_tensor(k.a_lo[:, KT - 1], k.q[:, KT - 1], k.a_hi[:, KT - 1].bitcast(F32), ALU.subtract).then_inc(z["h_lo"], 1)
            for u in range(1, 4):
                for j in range(2):
                    split(0, u, j, G)
            with dve.Fori(1, G) as g:
                for u in range(4):
                    for j in range(2):
                        split(g, u, j, G)

        @block.tensor
        def _(pe):
            pe.sem_inc(z["mm"], 8)
            pe.sem_inc(z["sqd"], 2)
            pe.sem_inc(z["x1"], 2)

            def group(g, first, ready):
                for u in range(4):
                    for j in range(2):
                        pe.wait_ge(z["lo"], 8 * g + (8 * first + 2 * u + j + 4))
                        if ready is not None:
                            pe.wait_ge(z[ready], 4 * u + 2 * j + 2)
                        for c in range(4):
                            if u + j == 0:
                                pe.wait_ge(z["ev"], 4 * g + (4 * first + c + 1))
                            for t in range(2):
                                w, kt = slice(t * 512 + c * P, t * 512 + (c + 1) * P), 4 * u + 2 * j + t
                                nc.tensor.matmul(p_out[c][:], w_hi[j][:, w], k.a_hi[:, kt], start=kt == 0, stop=False)
                                nc.tensor.matmul(p_out[c][:], w_hi[j][:, w], k.a_lo[:, kt], start=False, stop=False)
                                last = nc.tensor.matmul(p_out[c][:], w_lo[j][:, w], k.a_hi[:, kt], start=False, stop=kt == KT - 1)
                            last.then_inc(z["mm"], 1)

            def sums(g, start, stop):
                for c in range(4):
                    pe.wait_ge(z["sq"], 4 * g + c + 1)
                    nc.tensor.matmul(p_ss[:], k.ones[:], xsq[:, c % 2], start=start and c == 0, stop=stop and c == 3).then_inc(z["sqd"], 1)

            group(0, 0, "mix_lo")
            group(1, 0, None)
            sums(0, True, False)
            with pe.Fori(2, G) as g:
                group(g, 0, None)
                sums(g - 1, False, False)
            sums(G - 1, False, True)
            group(0, G, "h_lo")
            with pe.Fori(1, G) as g:
                group(g, G, None)


def retrieval(nc, k, dram):
    with ExitStack() as ctx:
        sb = lambda n, s, d=F32: ctx.enter_context(nc.sbuf_tensor(n, s, d))
        sem = lambda n: k.semaphore(nc, n)
        HJ = 2 * HEADS
        keys = sb("sub_keys", [P, HJ, NKEYS])
        s_sb = [sb(f"key_scores{s}", [P, HJ, NKEYS]) for s in range(2)]
        sv, si, sif = sb("key_best", [P, HJ, TOPK]), sb("key_index", [P, HJ, TOPK], U32), sb("key_index_f", [P, HJ, TOPK])
        cand = sb("candidates", [P, HEADS, TOPK * TOPK])
        best, ci = sb("best", [P, HEADS, TOPK]), sb("best_index", [P, HEADS, TOPK], U32)
        cab, cabf = sb("pair_index", [P, 2, HEADS * TOPK], U32), sb("pair_index_f", [P, 2, HEADS * TOPK])
        iota16 = sb("iota16", [P, TOPK])
        hot = [sb(f"pick{j}", [P, HEADS * TOPK, TOPK]) for j in range(2)]
        res = sb("picked", [P, 3, HEADS * TOPK])
        gsum, ginv = sb("softmax_sum", [P, HEADS]), sb("softmax_inv", [P, HEADS])
        ps = [ctx.enter_context(nc.psum_tensor(f"p_scores{s}", [P, HJ * NKEYS // 2], F32)) for s in range(2)]
        pt = ctx.enter_context(nc.psum_tensor("p_picked", [P, 512], F32))
        names = ("turn in s ev m1 i1 r1 m2 i2 sif cand cm1 ci1 cr1 cm2 ci2 ab abf eq pick red gd ge gs gi g tr tread")
        z = {n: sem("p4_" + n) for n in names.split()}
        block = ctx.enter_context(nc.Block())
        LOW = -3.0e38

        @block.sync
        def _(sp):
            sp.dma_start(keys[:], dram["sub_keys"]).then_inc(z["in"], 16)
            sp.dma_start(iota16[:], dram["iota"][:, 0:TOPK]).then_inc(z["in"], 16)

        @block.tensor
        def _(pe):
            pe.wait_ge(z["in"], 32)

            def scores(t):
                for j in range(HJ):
                    half, col = j // HEADS, j % HEADS
                    if col == 0 and t > 0:
                        pe.wait_ge(z["ev"], 2 * t - 1 + half)
                    last = nc.tensor.matmul(ps[half][:, col * NKEYS:(col + 1) * NKEYS], k.q[:, j, t * P:(t + 1) * P],
                                            keys[:, j], start=True, stop=True)
                    if col == HEADS - 1:
                        last.then_inc(z["s"], 1)

            pe.sem_inc(z["tr"], 1)
            scores(0)
            for t in range(LT):
                if t + 1 < LT:
                    scores(t + 1)
                pe.wait_ge(z["red"], 2 * t + 2)
                pe.wait_ge(z["g"], t + 1)
                if t > 0:
                    pe.wait_ge(z["tread"], t)
                for j in range(3):
                    last = nc.tensor.transpose(pt[:, j * P:(j + 1) * P], res[:, j], k.ident[:])
                last.then_inc(z["tr"], 1)

        @block.scalar
        def _(act):
            def evacuate(t, s, first):
                if not first:
                    act.wait_ge(z["i2"], t - 1)
                for half in range(2):
                    act.wait_ge(z["s"], 2 * t + (half + 1))
                    nc.scalar.activation(s_sb[s][:, half * HEADS:(half + 1) * HEADS], ps[half][:].rearrange("p (a n) -> p a n", n=NKEYS),
                                         ACT.Copy).then_inc(z["ev"], 1)

            def finish(t):
                act.wait_ge(z["gd"], t + 1)
                nc.scalar.activation(res[:, 2], res[:, 2], ACT.Exp).then_inc(z["ge"], 1)
                act.wait_ge(z["tr"], t + 2)
                nc.scalar.activation(k.picked[:, :, bass.ds(t * P, P)], pt[:, 0:3 * P].rearrange("p (j n) -> p j n", j=3), ACT.Copy).then_inc(z["tread"], 1)

            evacuate(0, 0, True)
            evacuate(1, 1, True)
            finish(0)
            evacuate(2, 0, False)
            finish(1)
            evacuate(3, 1, False)
            finish(2)
            finish(3)

        @block.vector
        def _(dve):
            v = nc.vector
            dve.wait_ge(z["in"], 32)

            def top16(t, tag, n, src, val, idx):
                for j in range(n):
                    last = v.max(val(j)[:, 0:8], src(j))
                last.then_inc(z[tag + "m1"], 1)
                dve.wait_ge(z[tag + "m1"], t + 1)
                dve.sem_inc(z["turn"], 1)
                for j in range(n):
                    last = v.max_index(idx(j)[:, 0:8], val(j)[:, 0:8], src(j))
                last.then_inc(z[tag + "i1"], 1)
                dve.wait_ge(z[tag + "i1"], t + 1)
                dve.sem_inc(z["turn"], 1)
                for j in range(n):
                    last = v.match_replace(src(j), val(j)[:, 0:8], src(j), LOW)
                last.then_inc(z[tag + "r1"], 1)
                dve.wait_ge(z[tag + "r1"], t + 1)
                dve.sem_inc(z["turn"], 1)
                for j in range(n):
                    last = v.max(val(j)[:, 8:16], src(j))
                last.then_inc(z[tag + "m2"], 1)
                dve.wait_ge(z[tag + "m2"], t + 1)
                dve.sem_inc(z["turn"], 1)
                for j in range(n):
                    last = v.max_index(idx(j)[:, 8:16], val(j)[:, 8:16], src(j))
                last.then_inc(z[tag + "i2"], 1)
                dve.wait_ge(z[tag + "i2"], t + 1)
                dve.sem_inc(z["turn"], 1)

            with dve.Fori(0, LT // 2) as tt:
                for s in range(2):
                    t = 2 * tt + s
                    dve.wait_ge(z["ev"], 2 * t + 2)
                    dve.sem_inc(z["turn"], 1)
                    top16(t, "", HJ, lambda j: s_sb[s][:, j], lambda j: sv[:, j], lambda j: si[:, j])
                    v.tensor_copy(sif[:], si[:]).then_inc(z["sif"], 1)
                    pair = sv[:].rearrange("p (h j) a -> p h j a", j=2)
                    shape = [P, HEADS, TOPK, TOPK]
                    v.tensor_tensor(cand[:].rearrange("p h (a b) -> p h a b", a=TOPK),
                                    pair[:, :, 0, :].rearrange("p h (a o) -> p h a o", o=1).to_broadcast(shape),
                                    pair[:, :, 1, :].rearrange("p h (o b) -> p h o b", o=1).to_broadcast(shape), ALU.add).then_inc(z["cand"], 1)
                    dve.wait_ge(z["cand"], t + 1)
                    dve.sem_inc(z["turn"], 1)
                    top16(t, "c", HEADS, lambda h: cand[:, h], lambda h: best[:, h], lambda h: ci[:, h])
                    flat = ci[:].rearrange("p h n -> p (h n)")
                    v.tensor_single_scalar(cab[:, 0], flat, 4, ALU.logical_shift_right)
                    v.tensor_single_scalar(cab[:, 1], flat, 15, ALU.bitwise_and).then_inc(z["ab"], 1)
                    dve.wait_ge(z["tr"], t + 1)
                    v.tensor_tensor(res[:, 2].rearrange("p (h n) -> p h n", n=TOPK), best[:], best[:, :, 0:1].to_broadcast([P, HEADS, TOPK]),
                                    ALU.subtract).then_inc(z["gd"], 1)
                    dve.wait_ge(z["ab"], t + 1)
                    v.tensor_copy(cabf[:], cab[:]).then_inc(z["abf"], 1)
                    dve.wait_ge(z["abf"], t + 1)
                    shape = [P, HEADS * TOPK, TOPK]
                    for j in range(2):
                        v.tensor_tensor(hot[j][:], cabf[:, j].rearrange("p (n o) -> p n o", o=1).to_broadcast(shape),
                                        iota16[:].rearrange("p (o a) -> p o a", o=1).to_broadcast(shape), ALU.is_equal).then_inc(z["eq"], 1)
                    for j in range(2):
                        dve.wait_ge(z["eq"], 2 * t + (j + 1))
                        by_head = hot[j][:].rearrange("p (h n) a -> p h n a", n=TOPK)
                        index = sif[:].rearrange("p (h j) (o a) -> p h j o a", j=2, o=1)[:, :, j]
                        v.tensor_tensor(by_head, by_head, index.to_broadcast([P, HEADS, TOPK, TOPK]), ALU.mult).then_inc(z["pick"], 1)
                    for j in range(2):
                        dve.wait_ge(z["pick"], 2 * t + (j + 1))
                        v.tensor_reduce(res[:, j], hot[j][:], AX.X, ALU.add).then_inc(z["red"], 1)
                    dve.wait_ge(z["ge"], t + 1)
                    w = res[:, 2].rearrange("p (h n) -> p h n", n=TOPK)
                    v.tensor_reduce(gsum[:], w, AX.X, ALU.add).then_inc(z["gs"], 1)
                    dve.wait_ge(z["gs"], t + 1)
                    v.reciprocal(ginv[:], gsum[:]).then_inc(z["gi"], 1)
                    dve.wait_ge(z["gi"], t + 1)
                    v.tensor_tensor(w, w, ginv[:].rearrange("p (h o) -> p h o", o=1).to_broadcast([P, HEADS, TOPK]), ALU.mult).then_inc(z["g"], 1)


def gate_matrix(nc, k, dram):
    with ExitStack() as ctx:
        sb = lambda n, s, d=F32: ctx.enter_context(nc.sbuf_tensor(n, s, d))
        sem = lambda n: k.semaphore(nc, n)
        QUAD = 4
        iota = sb("iota128", [P, NKEYS])
        hots = k.q[:].rearrange("p k n -> p (k n)")[:, 0:8 * QUAD * NKEYS].rearrange("p (s n a) -> p s n a", n=QUAD, a=NKEYS)
        hot1, hot2 = hots[:, 0:4], hots[:, 4:8]
        TB = 64
        gs = [sb(f"gate_block{s}", [P, NKEYS, TB]) for s in range(2)]
        pg = [ctx.enter_context(nc.psum_tensor(f"p_gate{s}", [P, 512], F32)) for s in range(4)]
        z = {n: sem("p5_" + n) for n in ("in", "hot1", "diff2", "hot2", "mm", "ev")}
        s_st = [sem(f"p5_stored{s}") for s in range(2)]
        block = ctx.enter_context(nc.Block())
        QB = TB // QUAD

        @block.sync
        def _(sp):
            sp.dma_start(iota[:], dram["iota"]).then_inc(z["in"], 16)
            with sp.Fori(0, SEQ // TB // 2) as b:
                for s in range(2):
                    sp.wait_ge(z["ev"], 2 * QB * b + (QB * (s + 1) + 4))
                    sp.dma_start(dram["gate"][:, :, bass.ds(2 * TB * b + TB * s, TB)].rearrange("a p n -> p a n"), gs[s][:]).then_inc(s_st[s], 16)
            for s in range(2):
                sp.wait_ge(s_st[s], 16 * (SEQ // TB // 2 + 1))

        @block.vector
        def _(dve):
            dve.wait_ge(z["in"], 16)
            with dve.Fori(0, SEQ // 16) as i:
                for s in range(4):
                    dve.wait_ge(z["mm"], 4 * i + s + 1)
                    for n in range(QUAD):
                        tok = bass.ds(16 * i + (4 * s + n), 1)
                        last = nc.vector.tensor_scalar(hot1[:, s, n], iota[:], k.picked[:, 0, tok], k.picked[:, 2, tok], ALU.is_equal, ALU.mult)
                    last.then_inc(z["hot1"], 1)
                    dve.wait_ge(z["diff2"], 4 * i + s + 1)
                    nc.vector.tensor_scalar(hot2[:, s], hot2[:, s], 0.0, None, ALU.is_equal).then_inc(z["hot2"], 1)

        @block.gpsimd
        def _(pool):
            pool.wait_ge(z["in"], 16)
            with pool.Fori(0, SEQ // 16) as i:
                for s in range(4):
                    pool.wait_ge(z["mm"], 4 * i + s + 1)
                    second = k.picked[:, 1, bass.ds(16 * i + 4 * s, QUAD)].rearrange("p (n o) -> p n o", o=1)
                    nc.gpsimd.tensor_tensor(hot2[:, s], second.to_broadcast([P, QUAD, NKEYS]),
                                            iota[:].rearrange("p (o a) -> p o a", o=1).to_broadcast([P, QUAD, NKEYS]),
                                            ALU.subtract).then_inc(z["diff2"], 1)

        @block.tensor
        def _(pe):
            pe.sem_inc(z["mm"], 4)
            with pe.Fori(0, SEQ // 16) as i:
                for s in range(4):
                    pe.wait_ge(z["hot1"], 4 * i + s + 1)
                    pe.wait_ge(z["hot2"], 4 * i + s + 1)
                    pe.wait_ge(z["ev"], 4 * i + s + 1)
                    for n in range(QUAD):
                        last = nc.tensor.matmul(pg[s][:, n * NKEYS:(n + 1) * NKEYS], hot2[:, s, n], hot1[:, s, n], start=True, stop=True)
                    last.then_inc(z["mm"], 1)

        @block.scalar
        def _(act):
            act.sem_inc(z["ev"], 4)
            act.sem_inc(s_st[0], 16)
            act.sem_inc(s_st[1], 16)
            with act.Fori(0, SEQ // TB // 2) as b:
                for r in range(2):
                    act.wait_ge(s_st[r], 16 * b + 16)
                    with act.Fori(0, QB // 4) as i:
                        for s in range(4):
                            act.wait_ge(z["mm"], 2 * QB * b + (QB * r + s + 5) + 4 * i)
                            out = gs[r][:, :, bass.ds(16 * i + 4 * s, QUAD)].rearrange("p a n -> p n a")
                            nc.scalar.activation(out, pg[s][:].rearrange("p (n a) -> p n a", n=QUAD), ACT.Copy).then_inc(z["ev"], 1)


def experts(nc, k, dram):
    with ExitStack() as ctx:
        sb = lambda n, s, d=F32: ctx.enter_context(nc.sbuf_tensor(n, s, d))
        pb = lambda n: ctx.enter_context(nc.psum_tensor(n, [P, 512], F32))
        sem = lambda n: k.semaphore(nc, n)
        HT = TILE // 2
        free = k.q[:].rearrange("p k n -> p (k n)")
        u_st = [free[:, s * HT:(s + 1) * HT] for s in range(2)]
        v_st = [free[:, s * HT:(s + 1) * HT] for s in range(2, 4)]
        u_hi, u_lo = [sb(f"u_hi{s}", [P, HT], F32R) for s in range(4)], [sb(f"u_lo{s}", [P, HT], F32R) for s in range(4)]
        v_hi, v_lo = [sb(f"v_hi{s}", [P, HT], F32R) for s in range(4)], [sb(f"v_lo{s}", [P, HT], F32R) for s in range(4)]
        gt = [free[:, 4 * HT + s * SEQ:4 * HT + (s + 1) * SEQ] for s in range(2)]
        af = [free[:, 4 * HT + s * SEQ:4 * HT + (s + 1) * SEQ] for s in range(2, 4)]
        a_hi, a_lo = [sb(f"act_hi{s}", [P, SEQ], F32R) for s in range(2)], [sb(f"act_lo{s}", [P, SEQ], F32R) for s in range(2)]
        pu, pv = [pb(f"p_u{s}") for s in range(2)], [pb(f"p_v{s}") for s in range(6)]
        names = "u_hi u_lo v_hi v_lo umm vmm act ga ahi alo ev"
        z = {n: sem("p6_" + n) for n in names.split()}
        s_u, s_v, s_g = ([sem(f"p6_{n}_in{s}") for s in range(2)] for n in "uvg")
        block = ctx.enter_context(nc.Block())
        N = E_TILES // PAIR
        def pairs(eng):
            with eng.Fori(0, N - 1) as i:
                yield i, False
            yield N - 1, True

        u_src = lambda i, j: dram["u"][bass.ds(2 * i + j // 2, 1), :, (j % 2) * HT:(j % 2 + 1) * HT].rearrange("a p n -> (a p) n")
        v_src = lambda i, j: dram["v"][bass.ds(2 * i + j % 2, 1), :, (j // 2) * HT:(j // 2 + 1) * HT].rearrange("a p n -> (a p) n")

        @block.sync
        def _(sp):
            def load_u(i, j, first=False):
                if not (first and j < 2):
                    sp.wait_ge(z["u_lo"], 4 * i + (j - 1))
                sp.dma_start(u_st[j % 2], u_src(i, j)).then_inc(s_u[j % 2], 16)

            for j in range(4):
                load_u(0, j, True)
            for i, last_pair in pairs(sp):
                for j in range(4):
                    sp.wait_ge(z["v_lo"], 4 * i + (j + 1))
                    sp.dma_start(v_st[j % 2], v_src(i, j)).then_inc(s_v[j % 2], 16)
                    if j < 2:
                        sp.wait_ge(z["ga"], 2 * i + (j + 1))
                        sp.dma_start(gt[j], dram["gate"][bass.ds(2 * i + j, 1)].rearrange("a p n -> (a p) n")).then_inc(s_g[j], 16)
                if not last_pair:
                    for j in range(4):
                        load_u(i + 1, j)

        @block.scalar
        def _(act):
            def u_high(i, j):
                act.wait_ge(s_u[j % 2], 32 * i + 16 * (j // 2) + 16)
                act.wait_ge(z["umm"], 4 * i + (j + 1))
                nc.scalar.activation(u_hi[j][:], u_st[j % 2], ACT.Copy).then_inc(z["u_hi"], 1)

            def v_high(i, j):
                act.wait_ge(s_v[j % 2], 32 * i + 16 * (j // 2) + 16)
                act.wait_ge(z["vmm"], 16 * i + (8 * (j // 2) + 8))
                nc.scalar.activation(v_hi[j][:], v_st[j % 2], ACT.Copy).then_inc(z["v_hi"], 1)

            def gelu(i, a):
                act.wait_ge(z["umm"], 4 * i + (2 * a + 6))
                act.wait_ge(z["alo"], 2 * i + (a + 1))
                nc.scalar.activation(af[a], pu[a][:], ACT.Gelu).then_inc(z["act"], 1)

            act.sem_inc(z["act"], 2)
            for j in range(4):
                u_high(0, j)
            for i, last_pair in pairs(act):
                v_high(i, 0)
                v_high(i, 1)
                gelu(i, 0)
                v_high(i, 2)
                v_high(i, 3)
                gelu(i, 1)
                for j in range(0 if last_pair else 4):
                    u_high(i + 1, j)

        @block.vector
        def _(dve):
            v = nc.vector
            dve.sem_inc(z["v_lo"], 2)
            dve.sem_inc(z["ga"], 2)
            dve.sem_inc(z["alo"], 2)
            dve.sem_inc(z["ev"], 4)

            def u_low(i, j):
                dve.wait_ge(z["u_hi"], 4 * i + (j + 1))
                v.tensor_tensor(u_lo[j][:], u_st[j % 2], u_hi[j][:].bitcast(F32), ALU.subtract).then_inc(z["u_lo"], 1)

            def v_low(i, j):
                dve.wait_ge(z["v_hi"], 4 * i + (j + 1))
                v.tensor_tensor(v_lo[j][:], v_st[j % 2], v_hi[j][:].bitcast(F32), ALU.subtract).then_inc(z["v_lo"], 1)

            def weigh(i, a):
                dve.wait_ge(z["act"], 2 * i + (a + 3))
                dve.wait_ge(s_g[a], 16 * i + 16)
                dve.wait_ge(z["vmm"], 16 * i + 16)
                v.tensor_tensor(af[a], af[a], gt[a], ALU.mult).then_inc(z["ga"], 1)
                dve.wait_ge(z["ga"], 2 * i + (a + 3))
                v.tensor_copy(a_hi[a][:], af[a]).then_inc(z["ahi"], 1)
                dve.wait_ge(z["ahi"], 2 * i + (a + 1))
                v.tensor_tensor(a_lo[a][:], af[a], a_hi[a][:].bitcast(F32), ALU.subtract).then_inc(z["alo"], 1)

            for j in range(4):
                u_low(0, j)
            for i, last_pair in pairs(dve):
                v_low(i, 0)
                v_low(i, 1)
                weigh(i, 0)
                v_low(i, 2)
                v_low(i, 3)
                weigh(i, 1)
                for m in range(KT):
                    dve.wait_ge(z["vmm"], 16 * i + (m + 17))
                    v.scalar_tensor_tensor(k.x[:, m], pv[m % 6][:], k.mod2[:, 3 * KT + m:3 * KT + m + 1], k.x[:, m], ALU.mult, ALU.add).then_inc(z["ev"], 1)
                    if m % 4 == 1 and not last_pair:
                        u_low(i + 1, m // 4)

        @block.tensor
        def _(pe):
            pe.sem_inc(z["umm"], 4)
            pe.sem_inc(z["vmm"], 16)
            with pe.Fori(0, N) as i:
                for j in range(4):
                    a = j // 2
                    pe.wait_ge(z["u_lo"], 4 * i + (j + 1))
                    if j % 2 == 0:
                        pe.wait_ge(z["act"], 2 * i + (a + 1))
                    for t in range(KT // 2):
                        w, kt = slice(t * P, (t + 1) * P), (j % 2) * (KT // 2) + t
                        nc.tensor.matmul(pu[a][:], u_hi[j][:, w], k.a_hi[:, kt], start=kt == 0, stop=False)
                        nc.tensor.matmul(pu[a][:], u_hi[j][:, w], k.a_lo[:, kt], start=False, stop=False)
                        last = nc.tensor.matmul(pu[a][:], u_lo[j][:, w], k.a_hi[:, kt], start=False, stop=kt == KT - 1)
                    last.then_inc(z["umm"], 1)
                first = [(m, a) for a in range(PAIR) for m in range(6)]
                for m, a in first + [(m, a) for m in range(6, KT) for a in range(PAIR)]:
                    j = 2 * (m // 8) + a
                    w = slice(m % 8 * P, (m % 8 + 1) * P)
                    if m % 8 == 0:
                        pe.wait_ge(z["v_lo"], 4 * i + (j + 3))
                    if m == 0:
                        pe.wait_ge(z["alo"], 2 * i + (a + 3))
                    if a == 0 and m < 4:
                        pe.wait_ge(z["ev"], 16 * i + (m + 1))
                    if a == 0 and m >= 6:
                        pe.wait_ge(z["ev"], 16 * i + (m - 1))
                    nc.tensor.matmul(pv[m % 6][:], v_hi[j][:, w], a_hi[a][:], start=a == 0, stop=False)
                    nc.tensor.matmul(pv[m % 6][:], v_hi[j][:, w], a_lo[a][:], start=False, stop=False)
                    last = nc.tensor.matmul(pv[m % 6][:], v_lo[j][:, w], a_hi[a][:], start=False, stop=a == PAIR - 1)
                    if a == PAIR - 1:
                        last.then_inc(z["vmm"], 1)


def final_norm(nc, k, dram):
    with ExitStack() as ctx:
        sb = lambda n, s, d=F32: ctx.enter_context(nc.sbuf_tensor(n, s, d))
        sem = lambda n: k.semaphore(nc, n)
        fg, rstd, xsq = sb("final_g", [P, KT]), sb("rstd3", [P, SEQ]), sb("x2_sq", [P, KT, SEQ])
        ss = ctx.enter_context(nc.psum_tensor("ss3", [P, SEQ], F32))
        z = {n: sem("p7_" + n) for n in ("in", "sq", "ss", "ln", "rstd", "y", "st")}
        block = ctx.enter_context(nc.Block())

        @block.sync
        def _(sp):
            sp.dma_start(fg[:], dram["final_norm_g"]).then_inc(z["in"], 16)
            for q in range(4):
                sp.wait_ge(z["y"], 4 * q + 4)
                sp.dma_start(dram["out"][:, 4 * q:4 * q + 4], xsq[:, 4 * q:4 * q + 4]).then_inc(z["st"], 16)
            sp.wait_ge(z["st"], 64)

        @block.scalar
        def _(act):
            for t in range(KT):
                nc.scalar.activation(xsq[:, t], k.x[:, t], ACT.Square).then_inc(z["sq"], 1)
            act.wait_ge(z["ss"], 1)
            nc.scalar.activation(rstd[:], ss[:], ACT.Ln, bias=k.eps[:], scale=1.0 / D).then_inc(z["ln"], 1)
            act.wait_ge(z["ln"], 1)
            nc.scalar.activation(rstd[:], rstd[:], ACT.Exp, scale=-0.5).then_inc(z["rstd"], 1)

        @block.tensor
        def _(pe):
            for t in range(KT):
                pe.wait_ge(z["sq"], t + 1)
                last = nc.tensor.matmul(ss[:], k.ones[:], xsq[:, t], start=t == 0, stop=t == KT - 1)
            last.then_inc(z["ss"], 1)

        @block.vector
        def _(dve):
            dve.wait_ge(z["in"], 16)
            dve.wait_ge(z["rstd"], 1)
            for t in range(KT):
                nc.vector.scalar_tensor_tensor(xsq[:, t], k.x[:, t], fg[:, t:t + 1], rstd[:], ALU.mult, ALU.mult).then_inc(z["y"], 1)


class Shared:

    def __init__(self):
        self.semaphores = []

    def semaphore(self, nc, name):
        self.semaphores.append(nc.alloc_semaphore(name=name))
        return self.semaphores[-1]

    def clear_semaphores(self, nc):
        nc.all_engine_barrier()
        nc.clear_and_free_semaphores(self.semaphores)
        nc.all_engine_barrier()
        self.semaphores = []


def program(nc, dram, upto=99):
    with ExitStack() as ctx:
        k = Shared()
        sb = lambda n, s, d=F32: ctx.enter_context(nc.sbuf_tensor(n, s, d))
        k.ident = sb("ident", [P, P])
        k.ones = sb("ones", [P, P])
        k.eps = sb("eps", [P, 1])
        k.c_act = sb("c_act", [P, KT, 2])
        k.mod2 = sb("mod2", [P, ADA - ADA1])
        with ExitStack() as c1:
            k.h_hi = c1.enter_context(nc.sbuf_tensor("h_hi", [P, KT, TOK], F32R))
            k.h_lo = c1.enter_context(nc.sbuf_tensor("h_lo", [P, KT, TOK], F32R))
            adaln_and_norm(nc, k, dram)
            input_projection(nc, k, dram)
        k.mix = k.q = sb("mix_then_query", [P, KT, SEQ])
        mixers(nc, k, dram)
        k.clear_semaphores(nc)
        if upto == 2:
            return dump(nc, k.mix, dram["out"])
        k.x, k.a_hi, k.a_lo = sb("x", [P, KT, SEQ]), sb("h2_hi", [P, KT, SEQ], F32R), sb("h2_lo", [P, KT, SEQ], F32R)
        output_and_query(nc, k, dram)
        if upto == 3:
            return dump(nc, k.q, dram["out"])
        with ExitStack() as c1:
            k.picked = c1.enter_context(nc.sbuf_tensor("picked_t", [P, 3, SEQ], F32))
            retrieval(nc, k, dram)
            if upto == 4:
                return dump(nc, k.picked, dram["out"][:, 0:3])
            gate_matrix(nc, k, dram)
        if upto == 5:
            return
        experts(nc, k, dram)
        final_norm(nc, k, dram)


def dump(nc, src, dst):
    with nc.semaphore("dump") as s, nc.Block() as block:
        @block.sync
        def _(sp):
            sp.dma_start(dst, src[:]).then_inc(s, 16)
            sp.wait_ge(s, 16)


def columns(v, n):
    return np.ascontiguousarray(np.asarray(v).reshape(n, P).T)


def tiles(w):
    w = np.asarray(w)
    n = w.shape[1] // P
    return np.ascontiguousarray(w.reshape(KT, P, n, P).transpose(2, 1, 0, 3)).reshape(n, P, KT * P)


def groups_of_512(w):
    w = np.asarray(w)
    n = w.shape[1] // 512
    return np.ascontiguousarray(w.reshape(KT, P, n, 512).transpose(2, 1, 0, 3)).reshape(n, P, KT * 512)


def features(x):
    x = np.asarray(x)
    return np.ascontiguousarray(x.reshape(x.shape[0], KT, P).transpose(2, 1, 0))


def rope_tables():
    tok, feat = np.arange(SEQ), np.arange(P)
    n_freq = 16
    inv = 10000.0 ** (-np.arange(n_freq, dtype=np.float32) / n_freq)
    pos = np.where((feat % 64 < 32)[:, None], (tok // 64)[None, :], (tok % 64)[None, :]).astype(np.float32)
    ang = pos * inv.astype(np.float32)[feat % 16][:, None]
    first = feat % 32 < 16
    partner = np.where(first, feat + 16, feat - 16)
    perm = np.zeros((P, P), np.float32)
    perm[partner, feat] = 1.0
    sin = np.where(first[:, None], -np.sin(ang), np.sin(ang))
    return perm, np.cos(ang).astype(np.float32), sin.astype(np.float32)


def level_masks():
    s, t = np.arange(P)[:, None], np.arange(P)[None, :]
    out = [((s // (2 * L) == t // (2 * L)) & (s // L != t // L)) for L in (P >> (l + 1) for l in range(LEVELS))]
    return np.ascontiguousarray(np.stack(out, axis=1).astype(np.float32))


def layout(inputs):
    a = {}
    a["x"] = features(inputs["x"][0])
    a["ctx"] = features(inputs["ctx"][0])
    a["c"] = np.ascontiguousarray(np.stack([columns(inputs["c"][0], KT), columns(inputs["c_ctx"], KT)], axis=2))
    order = np.arange(ADA // 4)
    order[:ADA1 // 4] = order[:ADA1 // 4].reshape(2, KT // 4).T.reshape(-1)
    a["w_ada"] = groups_of_512(inputs["w_ada"][0])[order]
    a["b_ada"] = np.ascontiguousarray(columns(inputs["b_ada"][0], ADA).reshape(P, ADA // 4, 4)[:, order].reshape(P, ADA))
    a["norm1_g"] = columns(inputs["norm1_g"][0], KT)
    w_in = inputs["w_in"][0].reshape(D, 8, HEADS * P)[:, list(PART_OF)].reshape(D, 8 * HEADS * P)
    a["w_in"] = groups_of_512(w_in)
    a["ident"] = np.eye(P, dtype=np.float32)
    g = np.asarray(inputs["hg_gamma"])
    a["hg_gamma"] = np.ascontiguousarray(g.reshape(2, 2, HEADS, P).transpose(3, 0, 1, 2))
    a["hg_norm_g"] = columns(inputs["hg_norm_g"][0], HEADS)
    a["da_subln_g"] = columns(inputs["da_subln_g"][0], HEADS)
    a["da_lambda"] = np.stack([inputs["da_lambda_" + n][0] for n in ("q1", "q2", "k1", "k2")])[None]
    a["rope_perm"], a["rope_cos"], a["rope_sin"] = rope_tables()
    a["level_masks"] = level_masks()
    a["w_out"] = groups_of_512(inputs["w_out"][0])
    a["norm2_g"] = columns(inputs["norm2_g"][0], KT)
    a["w_query"] = groups_of_512(inputs["peer_w_query"][0])
    a["sub_keys"] = np.ascontiguousarray(np.asarray(inputs["peer_sub_keys"][0]).reshape(2 * HEADS, NKEYS, P).transpose(2, 0, 1))
    a["iota"] = np.tile(np.arange(NKEYS, dtype=np.float32), (P, 1))
    a["u"] = tiles(np.asarray(inputs["peer_u"][0]).T)
    a["v"] = np.asarray(inputs["peer_v"][0]).reshape(E_TILES, P, D)
    a["final_norm_g"] = columns(inputs["final_norm_g"], KT)
    return a


def kernel(**inputs):
    import concourse.bacc as bacc
    from concourse.bass_utils import run_bass_kernel_spmd

    nc = bacc.Bacc("TRN2", target_bir_lowering=False, num_devices=1)
    arrays = {f"in_{name}": a for name, a in layout(inputs).items()}
    dram = {name[3:]: nc.dram_tensor(name, a.shape, mybir.dt.from_np(a.dtype), kind="ExternalInput").ap() for name, a in arrays.items()}
    dram["out"] = nc.dram_tensor("y_features", (P, KT, SEQ), F32, kind="ExternalOutput").ap()
    for name, shape in (("proj_lat", (IN_TILES, P, SEQ)), ("proj_ctx", (5, CT, P, HEADS * P)), ("gate", (NKEYS, NKEYS, SEQ))):
        dram[name] = nc.dram_tensor(name, shape, F32, kind="Internal").ap()
    program(nc, dram)
    r = run_bass_kernel_spmd(nc, [arrays], core_ids=[0])
    y = np.asarray(r.results[0]["y_features"])
    return np.ascontiguousarray(y.transpose(2, 1, 0)).reshape(1, SEQ, D)
```

```python
import math
from contextlib import ExitStack

import numpy as np
import concourse.bass as bass
from concourse import mybir

F32 = mybir.dt.float32
F32R = mybir.dt.float32r
U8 = mybir.dt.uint8
U32 = mybir.dt.uint32
ALU = mybir.AluOpType
ACT = mybir.ActivationFunctionType
AX = mybir.AxisListType

P = 128
D = 2048
KT = D // P
SEQ = 512
CTX = 256
TOK = CTX + SEQ
HEADS = 8
EPS = 1e-6
ADA1 = 2 * KT
ADA = 6 * KT
UNIT = 4 * 512
TILE = KT * P
LATENT_TILES = 3 * HEADS
IN_TILES = 8 * HEADS
HG_Q, HG_G, DA_Q, HG_FF, HG_FB, HG_I, DA_K, DA_V = range(8)
NT = TOK // P
CT = CTX // P
LT = SEQ // P
LEVELS = 7
PART_OF = (0, 4, 5, 1, 2, 3, 6, 7)
LAM_INIT = 0.8 - 0.6 * math.exp(0.0)
TOPK = 16
NKEYS = 128
E_TILES = NKEYS
PAIR = 2
EARLY_OF = (3, 2, 2, 2)
EARLY = sum(EARLY_OF)
TB = 64
HT = TILE // 2


def adaln_and_norm(nc, k, dram):
    with ExitStack() as ctx:
        sb = lambda n, s, d=F32: ctx.enter_context(nc.sbuf_tensor(n, s, d))
        pb = lambda n: ctx.enter_context(nc.psum_tensor(n, [P, 512], F32))
        sem = lambda n: k.semaphore(nc, n)
        x = sb("x0", [P, KT, TOK])
        xsq = sb("x0_sq", [P, 2, TOK])
        stage = [sb(f"ada_stage{s}", [P, UNIT]) for s in range(4)]
        b_ada = sb("b_ada0", [P, ADA1])
        g1 = sb("norm1_g", [P, KT])
        csig = sb("c_sig", [P, KT, 2])
        craw = sb("c_raw", [P, KT, 2])
        row = sb("ada_row", [2, ADA1 * P])
        mod = sb("mod1", [P, ADA1, 2])
        gain = sb("gain1", [P, KT, 2])
        rstd = sb("rstd1", [P, TOK])
        ss_lat, ss_ctx, p_row, p_col = pb("ss_lat"), pb("ss_ctx"), [pb(f"p_ada_row{s}") for s in range(2)], pb("p_ada_col")
        s_small, s_x = sem("p0_small_in"), [sem(f"p0_x_in{n}") for n in range(4)]
        s_ada = [sem(f"p0_ada_in{s}") for s in range(4)]
        s_sig, s_cact, s_ones = sem("p0_c_sigmoid"), sem("p0_c_act"), sem("p0_ones")
        s_sq, s_sqd = sem("p0_squares"), sem("p0_squares_summed")
        s_adad, s_row, s_col = sem("p0_ada_units_used"), sem("p0_ada_row"), sem("p0_ada_columns")
        s_ln, s_rstd, s_xn, s_mod, s_gain = (sem("p0_ln"), sem("p0_rstd"), sem("p0_x_normed"), sem("p0_mod"),
                                             sem("p0_gain"))
        s_h, s_hi, s_lo = sem("p0_h"), sem("p0_h_hi"), sem("p0_h_lo")
        block = ctx.enter_context(nc.Block())
        chunks = ADA1 * P // 512
        shift_of = lambda t: t // 4 * 8 + t % 4

        @block.sync
        def _(sp):
            sp.dma_start(craw[:], dram["c"]).then_inc(s_small, 16)
            sp.dma_start(b_ada[:], dram["b_ada"][:, 0:ADA1]).then_inc(s_small, 16)
            sp.dma_start(g1[:], dram["norm1_g"]).then_inc(s_small, 16)
            sp.dma_start(k.ident[:], dram["ident"]).then_inc(s_small, 16)

            def load(c):
                for s in range(4):
                    sp.wait_ge(s_adad, 4 * c + s + 1)
                    sp.dma_start(stage[s][:], dram["w_ada"][bass.ds(c, 1), :, s * UNIT:(s + 1) * UNIT].rearrange("a p n -> (a p) n")).then_inc(s_ada[s], 16)

            load(0)
            for n in range(4):
                quarter = slice(n * KT // 4, (n + 1) * KT // 4)
                sp.dma_start(x[:, quarter, 0:CTX], dram["ctx"][:, quarter]).then_inc(s_x[n], 16)
                sp.dma_start(x[:, quarter, CTX:TOK], dram["x"][:, quarter]).then_inc(s_x[n], 16)
            with sp.Fori(1, chunks) as c:
                load(c)

        @block.gpsimd
        def _(pool):
            nc.gpsimd.memset(k.ones[:], 1.0).then_inc(s_ones, 1)
            nc.gpsimd.memset(k.eps[:], EPS).then_inc(s_ones, 1)

        @block.scalar
        def _(act):
            act.wait_ge(s_small, 64)
            nc.scalar.activation(csig[:], craw[:], ACT.Sigmoid).then_inc(s_sig, 1)
            for t in range(KT):
                if t % (KT // 4) == 0:
                    act.wait_ge(s_x[4 * t // KT], 32)
                if t >= 2:
                    act.wait_ge(s_sqd, t - 1)
                nc.scalar.activation(xsq[:, t % 2, :], x[:, t, :], ACT.Square).then_inc(s_sq, 1)
            act.wait_ge(s_ones, 2)
            act.wait_ge(s_sqd, KT)
            nc.scalar.activation(rstd[:, 0:CTX], ss_ctx[:, 0:CTX], ACT.Ln, bias=k.eps[:], scale=1.0 / D).then_inc(s_ln, 1)
            nc.scalar.activation(rstd[:, CTX:TOK], ss_lat[:], ACT.Ln, bias=k.eps[:], scale=1.0 / D).then_inc(s_ln, 1)
            act.wait_ge(s_ln, 2)
            nc.scalar.activation(rstd[:], rstd[:], ACT.Exp, scale=-0.5).then_inc(s_rstd, 1)
            for t in range(KT):
                act.wait_ge(s_xn, t + 1)
                act.wait_ge(s_gain, t // 4 + 1)
                for j, (a, b) in enumerate(((CTX, TOK), (0, CTX))):
                    nc.scalar.activation(x[:, t, a:b], x[:, t, a:b], ACT.Identity, bias=mod[:, shift_of(t), j:j + 1],
                                         scale=gain[:, t, j:j + 1]).then_inc(s_h, 1)

        @block.vector
        def _(dve):
            dve.sem_inc(s_row, 2)
            dve.wait_ge(s_sig, 1)
            nc.vector.tensor_tensor(k.c_act[:], craw[:], csig[:], ALU.mult).then_inc(s_cact, 1)
            dve.wait_ge(s_rstd, 1)

            def split(t):
                dve.wait_ge(s_h, 2 * t + 2)
                nc.vector.tensor_copy(k.h_hi[:, t, :], x[:, t, :]).then_inc(s_hi, 1)
                dve.wait_ge(s_hi, t + 1)
                nc.vector.tensor_tensor(k.h_lo[:, t, :], x[:, t, :], k.h_hi[:, t, :].bitcast(F32), ALU.subtract).then_inc(s_lo, 1)

            for p in range(chunks // 2):
                quarter = range(4 * p, 4 * p + 4)
                for t in quarter:
                    nc.vector.tensor_tensor(x[:, t, :], x[:, t, :], rstd[:], ALU.mult).then_inc(s_xn, 1)
                for c in range(2 * p, 2 * p + 2):
                    dve.wait_ge(s_adad, 4 * c + 8)
                    nc.vector.tensor_copy(row[:, c * 512:(c + 1) * 512], p_row[c % 2][0:2, :]).then_inc(s_row, 1)
                dve.wait_ge(s_col, p + 1)
                cols = p_col[:, 16 * p:16 * p + 16].rearrange("p (a j) -> p a j", j=2)
                for j in range(2):
                    last = nc.vector.tensor_tensor(mod[:, 8 * p:8 * p + 8, j], cols[:, :, j], b_ada[:, 8 * p:8 * p + 8], ALU.add)
                last.then_inc(s_mod, 1)
                dve.wait_ge(s_mod, p + 1)
                for j in range(2):
                    last = nc.vector.scalar_tensor_tensor(gain[:, 4 * p:4 * p + 4, j], mod[:, 8 * p + 4:8 * p + 8, j], 1.0,
                                                          g1[:, 4 * p:4 * p + 4], ALU.add, ALU.mult)
                last.then_inc(s_gain, 1)
                for t in quarter:
                    split(t)

        @block.tensor
        def _(pe):
            pe.sem_inc(s_adad, 4)
            pe.wait_ge(s_ones, 2)
            def chunk(c):
                pe.wait_ge(s_row, c + 1)
                for s in range(4):
                    pe.wait_ge(s_ada[s], 16 * c + 16)
                    for t in range(4):
                        last = nc.tensor.matmul(p_row[c % 2][0:2, :], k.c_act[:, 4 * s + t, :], stage[s][:, t * 512:(t + 1) * 512],
                                                start=s + t == 0, stop=s + t == 6)
                    last.then_inc(s_adad, 1)

            pe.wait_ge(s_cact, 1)
            chunk(0)
            for t in range(KT):
                pe.wait_ge(s_sq, t + 1)
                nc.tensor.matmul(ss_ctx[:, 0:CTX], k.ones[:], xsq[:, t % 2, 0:CTX], start=t == 0, stop=t == KT - 1)
                nc.tensor.matmul(ss_lat[:], k.ones[:], xsq[:, t % 2, CTX:TOK], start=t == 0, stop=t == KT - 1).then_inc(s_sqd, 1)
            for p in range(chunks // 2):
                for c in range(2 * p, 2 * p + 2):
                    if c > 0:
                        chunk(c)
                pe.wait_ge(s_row, 2 * p + 4)
                if p >= 1:
                    pe.wait_ge(s_mod, p)
                for t in range(8 * p, 8 * p + 8):
                    last = nc.tensor.matmul(p_col[:, 2 * t:2 * t + 2], row[:, t * P:(t + 1) * P], k.ident[0:2, 0:2],
                                            start=True, stop=True)
                last.then_inc(s_col, 1)


def input_projection(nc, k, dram):
    with ExitStack() as ctx:
        sb = lambda n, s, d=F32: ctx.enter_context(nc.sbuf_tensor(n, s, d))
        pb = lambda n: ctx.enter_context(nc.psum_tensor(n, [P, 512], F32))
        sem = lambda n: k.semaphore(nc, n)
        stage = [sb(f"win_stage{s}", [P, UNIT]) for s in range(2)]
        w_hi = [sb(f"win_hi{s}", [P, UNIT], F32R) for s in range(2)]
        w_lo = [sb(f"win_lo{s}", [P, UNIT], F32R) for s in range(2)]
        ada = [sb(f"ada2_stage{s}", [P, UNIT]) for s in range(2)]
        acc = [sb(f"ada2_acc{s}", [P, 512]) for s in range(2)]
        out = sb("proj_out", [P, 6, 512])
        b_ada = sb("b_ada1", [P, ADA - ADA1])
        p_lat, p_ctx, p_mod = [pb(f"proj_lat{s}") for s in range(4)], [pb(f"proj_ctx{s}") for s in range(2)], pb("p_ada1")
        s_w = [sem(f"p1_w_in{s}") for s in range(2)]
        s_a = [sem(f"p1_ada_in{s}") for s in range(2)]
        s_b = sem("p1_bias_in")
        s_hi, s_lo, s_mm, s_acc, s_modp, s_mod = (sem("p1_w_hi"), sem("p1_w_lo"), sem("p1_units_multiplied"),
                                                  sem("p1_ada_steps"), sem("p1_ada_columns"), sem("p1_mod"))
        s_evl, s_evc = sem("p1_lat_banks_read"), sem("p1_ctx_banks_read")
        s_st = [sem("p1_lat_stored"), sem("p1_ctx_stored")]
        block = ctx.enter_context(nc.Block())
        groups = IN_TILES // 4
        lat_groups = LATENT_TILES // 4
        loops = ((0, lat_groups, False), (lat_groups, groups, True))
        credit = 5

        def blocks(g, u, context):
            per_unit = 6 if context else 4
            return 4 * per_unit * g + (per_unit * u + credit - (8 * lat_groups if context else 0))


        @block.sync
        def _(sp):
            sp.dma_start(b_ada[:], dram["b_ada"][:, ADA1:ADA]).then_inc(s_b, 16)
            with sp.Fori(0, groups) as g:
                for u in range(4):
                    sp.wait_ge(s_lo, 4 * g + u + 1)
                    sp.dma_start(stage[u % 2][:], dram["w_in"][bass.ds(g, 1), :, u * UNIT:(u + 1) * UNIT].rearrange("a p n -> (a p) n")).then_inc(s_w[u % 2], 16)
                    sp.wait_ge(s_acc, 16 * g + 4 * u + 4)
                    sp.dma_start(ada[u % 2][:], dram["w_ada"][bass.ds(g + ADA1 // 4, 1), :, u * UNIT:(u + 1) * UNIT].rearrange("a p n -> (a p) n")).then_inc(s_a[u % 2], 16)

        @block.scalar
        def _(act):
            act.sem_inc(s_evl, 4)
            act.sem_inc(s_evc, 2)
            act.sem_inc(s_mod, 1)
            act.sem_inc(s_st[0], 64)
            act.sem_inc(s_st[1], 32)
            act.wait_ge(s_b, 16)
            for a, b, context in loops:
                with act.Fori(a // 2, b // 2) as gg:
                    for q in range(2):
                        g = 2 * gg + q
                        for c in range(4):
                            act.wait_ge(s_st[0], 64 * g + 64)
                            act.wait_ge(s_mm, blocks(g, 3, context) + (c + 1))
                            nc.scalar.activation(out[:, c, :], p_lat[c][:], ACT.Copy).then_inc(s_evl, 1)
                            act.wait_ge(s_evl, 4 * g + (c + 5))
                            act.dma_start(dram["proj_lat"][bass.ds(4 * g + c, 1)].rearrange("a p n -> (a p) n"), out[:, c, :]).then_inc(s_st[0], 16)
                        for c in range(2 if context else 0):
                            act.wait_ge(s_st[1], 32 * (g - lat_groups) + 32)
                            act.wait_ge(s_mm, blocks(g, 3, context) + (c + 5))
                            nc.scalar.activation(out[:, 4 + c, :], p_ctx[c][:], ACT.Copy).then_inc(s_evc, 1)
                            act.wait_ge(s_evc, 2 * g + (c + 3 - 2 * lat_groups))
                            act.dma_start(dram["proj_ctx"][bass.ds(gg - lat_groups // 2, 1), c, :, q * 512:(q + 1) * 512].rearrange("a p n -> (a p) n"),
                                          out[:, 4 + c, :]).then_inc(s_st[1], 16)
                        act.wait_ge(s_modp, g + 3)
                        nc.scalar.activation(k.mod2[:, bass.ds(4 * g, 4)], p_mod[:, 0:4], ACT.Copy).then_inc(s_mod, 1)
            act.wait_ge(s_st[0], 64 * groups + 64)
            act.wait_ge(s_st[1], 32 * (groups - lat_groups) + 32)

        @block.vector
        def _(dve):
            dve.sem_inc(s_lo, 2)
            dve.sem_inc(s_acc, 8)
            for a, b, context in loops:
                with dve.Fori(a // 2, b // 2) as gg:
                    for q in range(2):
                        for u in range(4):
                            n, s = 8 * gg + (4 * q + u), u % 2
                            dve.wait_ge(s_w[s], 64 * gg + (32 * q + 16 * (u // 2) + 16))
                            dve.wait_ge(s_mm, blocks(2 * gg + q, u, context) - 4)
                            nc.vector.tensor_copy(w_hi[s][:], stage[s][:]).then_inc(s_hi, 1)
                            dve.wait_ge(s_hi, n + 1)
                            nc.vector.tensor_tensor(w_lo[s][:], stage[s][:], w_hi[s][:].bitcast(F32), ALU.subtract).then_inc(s_lo, 1)
                            dve.wait_ge(s_a[s], 64 * gg + (32 * q + 16 * (u // 2) + 16))
                            for t in range(4):
                                w = ada[s][:, t * 512:(t + 1) * 512]
                                c = k.c_act[:, 4 * u + t, 0:1]
                                dve.wait_ge(s_acc, 4 * n + (t + 8))
                                if u + t == 0:
                                    dve.wait_ge(s_modp, 2 * gg + (q + 1))
                                    nc.vector.tensor_scalar(acc[q][:], w, c, None, ALU.mult).then_inc(s_acc, 1)
                                else:
                                    nc.vector.scalar_tensor_tensor(acc[q][:], w, c, acc[q][:], ALU.mult, ALU.add).then_inc(s_acc, 1)
            dve.wait_ge(s_b, 16)
            dve.wait_ge(s_mod, groups + 1)
            nc.vector.tensor_tensor(k.mod2[:], k.mod2[:], b_ada[:], ALU.add)

        @block.tensor
        def _(pe):
            pe.sem_inc(s_mm, credit)
            pe.sem_inc(s_modp, 2)
            for a, b, context in loops:
                with pe.Fori(a // 2, b // 2) as gg:
                    for q in range(2):
                        g = 2 * gg + q
                        for u in range(4):
                            s = u % 2
                            pe.wait_ge(s_lo, 4 * g + (u + 3))
                            for c in range(4):
                                if u == 0:
                                    pe.wait_ge(s_evl, 4 * g + (c + 1))
                                for t in range(4):
                                    w, kt, h = slice(t * 512 + c * P, t * 512 + (c + 1) * P), 4 * u + t, slice(CTX, TOK)
                                    nc.tensor.matmul(p_lat[c][:], w_hi[s][:, w], k.h_hi[:, kt, h], start=kt == 0, stop=False)
                                    nc.tensor.matmul(p_lat[c][:], w_hi[s][:, w], k.h_lo[:, kt, h], start=False, stop=False)
                                    last = nc.tensor.matmul(p_lat[c][:], w_lo[s][:, w], k.h_hi[:, kt, h], start=False, stop=kt == KT - 1)
                                last.then_inc(s_mm, 1)
                            for c in range(2 if context else 0):
                                if u == 0:
                                    pe.wait_ge(s_evc, 2 * g + (c + 1 - 2 * lat_groups))
                                for t in range(4):
                                    w, kt, h = slice(t * 512, (t + 1) * 512), 4 * u + t, slice(c * P, (c + 1) * P)
                                    nc.tensor.matmul(p_ctx[c][:], k.h_hi[:, kt, h], w_hi[s][:, w], start=kt == 0, stop=False)
                                    nc.tensor.matmul(p_ctx[c][:], k.h_lo[:, kt, h], w_hi[s][:, w], start=False, stop=False)
                                    last = nc.tensor.matmul(p_ctx[c][:], k.h_hi[:, kt, h], w_lo[s][:, w], start=False, stop=kt == KT - 1)
                                last.then_inc(s_mm, 1)
                        pe.wait_ge(s_acc, 16 * g + 24)
                        pe.wait_ge(s_mod, g + 1)
                        for c in range(4):
                            last = nc.tensor.matmul(p_mod[:, c:c + 1], acc[q][:, c * P:(c + 1) * P], k.ones[:, 0:1], start=True, stop=True)
                        last.then_inc(s_modp, 1)


def mixers(nc, k, dram):
    with ExitStack() as ctx:
        sb = lambda n, s, d=F32: ctx.enter_context(nc.sbuf_tensor(n, s, d))
        pb = lambda n, w: ctx.enter_context(nc.psum_tensor(n, [P, w], F32))
        sem = lambda n: k.semaphore(nc, n)
        lat = [sb(f"head_lat{s}", [P, 8, SEQ]) for s in range(2)]
        cx = [sb(f"head_ctx{s}", [P, 5, CT, P]) for s in range(2)]
        perm, cos, sin = sb("rope_perm", [P, P]), sb("rope_cos", [P, SEQ]), sb("rope_sin", [P, SEQ])
        masks = sb("level_masks", [P, LEVELS, P], U8)
        gamma, lamv = sb("gamma", [P, 2, 2, HEADS]), sb("lam_vectors", [P, 4, 64])
        hgn, dan = sb("hg_norm_g", [P, HEADS]), sb("da_subln_g", [P, HEADS])
        lb, omlb, gdiff = sb("lower_bound", [P, 2, HEADS]), sb("one_minus_lb", [P, 2, HEADS]), sb("gamma_diff", [P, 2, HEADS])
        lamp, lams, lame, neglam = sb("lam_prod", [P, 2, 64]), sb("lam_sums", [P, 2]), sb("lam_exp", [P, 2]), sb("neg_lam", [P, 1])
        sq, sg = sb("q_sigmoid", [P, SEQ]), sb("g_sigmoid", [P, SEQ])
        f = [sb(f"forget{d}", [P, TOK]) for d in range(2)]
        key = [sb(f"hg_key{d}", [P, TOK]) for d in range(2)]
        lf = [sb(f"log_forget{d}", [P, TOK]) for d in range(2)]
        cum = [sb(f"cum{d}", [P, NT, P + 1]) for d in range(2)]
        q, gate = sb("hg_query", [P, SEQ]), sb("hg_gate", [P, SEQ])
        kt, qt = sb("da_key", [P, TOK]), sb("da_query", [P, SEQ])
        ropet = sb("rope_tmp", [P, 2, SEQ])
        iv = [sb(f"i_v_tokens{s}", [P, 2, LT, P]) for s in range(2)]
        nmx, nb, sums, rinv, rlam = (sb("neg_max", [P, 8]), sb("exp_bias", [P, 8]), sb("exp_sums", [P, 8]),
                                     sb("exp_inv", [P, 8]), sb("lam_inv", [P, 4]))
        ex = [[sb(f"exp{c}_{s}", [P, TOK]) for s in range(2)] for c in range(2)]
        pt = [sb(f"prob_t{s}", [P, TOK]) for s in range(2)]
        sqd, sqh, rd, rh = sb("da_sq", [P, SEQ]), sb("hg_sq", [P, SEQ]), sb("da_rstd", [P, SEQ]), sb("hg_rstd", [P, SEQ])
        lev = [sb(f"level_operands{s}", [P, 2, SEQ]) for s in range(3)]
        mask_in = lev[0][:].rearrange("p a n -> p (a n)")[:, 0:LEVELS * P].rearrange("p (l n) -> p l n", n=P)
        diag, sc = sb("diag_key", [P, SEQ]), sb("intra_scores", [P, SEQ])
        kd = [sb(f"key_decayed{d}", [P, NT, P]) for d in range(2)]
        kdt = [sb(f"key_decayed_t{d}", [P, NT, P]) for d in range(2)]
        qi = [sb(f"query_decayed{d}", [P, LT, P]) for d in range(2)]
        dc = [sb(f"chunk_decay{d}", [P, NT]) for d in range(2)]
        st = [sb(f"states{d}", [P, 5, P]) for d in range(2)]
        hgo = sb("hg_out", [P, SEQ])
        A, B, C, E, F = pb("bank_a", 1024), pb("bank_b", 1024), pb("bank_c", 1024), pb("bank_e", 512), pb("bank_f", 512)

        names = ("const_in lam_steps ready done tctx sig tctx_read rot tlat tlat_read cos f_steps f key lf cum q gate "
                 "rope_tmp kq s mx nb e inv p_scaled p tp tp_read pv dsq dss dln drs diag x ex ab lv sc kda qia kde kd qie qi "
                 "turn tkd tkd_read dc u state o hsq hss hln hrs hmul")
        z = {n: sem("p2_" + n) for n in names.split()}
        s_in = [sem(f"p2_in{s}") for s in range(2)]
        block = ctx.enter_context(nc.Block())

        CREDITS = {"lv": 1, "o": 1, "s": 8, "gate": 1, "hmul": 1, "hln": 1}

        def heads(eng):
            with eng.Fori(0, HEADS // 2 - 1) as hh:
                for par in range(2):
                    yield hh, 2 * hh + par, par, (hh + (1 if par else 0), 2 * hh + (par + 1), 1 - par)
            for h in (HEADS - 2, HEADS - 1):
                yield h // 2, h, h % 2, ((h + 1) // 2, h + 1, (h + 1) % 2) if h + 1 < HEADS else None

        def W(eng, name, per_head, h, n):
            eng.wait_ge(z[name], per_head * h + (n + CREDITS.get(name, 0)))

        def cumv(c, L, off, n):
            v = cum[c][:, CT:NT, :]
            if off + P <= P + 1:
                v = cum[c][:, CT:NT, off:off + P].rearrange("p t (b r) -> p t b r", r=2 * L)
                return v[:, :, :, 0:n]
            v = cum[c][:, CT:NT, off - L:off - L + P].rearrange("p t (b r) -> p t b r", r=2 * L)
            return v[:, :, :, L:L + n]

        def halfv(ap, L, second):
            return ap.rearrange("p (t b s j) -> p t b s j", t=LT, s=2, j=L)[:, :, :, second, :]

        @block.sync
        def _(sp):
            for dst, name in ((perm, "rope_perm"), (cos, "rope_cos"), (sin, "rope_sin"),
                              (gamma, "hg_gamma"), (hgn, "hg_norm_g"), (dan, "da_subln_g")):
                sp.dma_start(dst[:], dram[name]).then_inc(z["const_in"], 16)
            sp.dma_start(mask_in, dram["level_masks"]).then_inc(z["const_in"], 16)
            sp.dma_start(lamv[:], dram["da_lambda"].to_broadcast([P, 4, 64])).then_inc(z["const_in"], 16)
            pl = dram["proj_lat"].rearrange("(a h) p n -> h p a n", a=8)
            pc = dram["proj_ctx"]
            for hh, h, par, _ in heads(sp):
                W(sp, "done", 1, h, 1)
                sp.dma_start(lat[par][:], pl[bass.ds(h, 1)].rearrange("o p a n -> (o p) a n")).then_inc(s_in[par], 16)
                for a in range(5):
                    sp.dma_start(cx[par][:, a], pc[a, :, :, bass.ds(P * h, P)].rearrange("c p n -> p c n")).then_inc(s_in[par], 16)

        IN = 96

        @block.gpsimd
        def _(pool):
            pool.wait_ge(z["const_in"], 128)

            def prologue(hh, h, par):
                pool.wait_ge(s_in[par], IN * hh + IN)
                W(pool, "s", 8, h, 0)
                nc.gpsimd.tensor_tensor(kt[:, CTX:TOK], lat[par][:, DA_K], cos[:], ALU.mult).then_inc(z["cos"], 1)
                nc.gpsimd.tensor_tensor(qt[:], lat[par][:, DA_Q], cos[:], ALU.mult).then_inc(z["cos"], 1)

            prologue(0, 0, 0)
            for hh, h, par, after in heads(pool):
                W(pool, "cum", 2, h, 2)
                for l in range(LEVELS):
                    L = P >> (l + 1)
                    nb_ = P // (2 * L)
                    W(pool, "lv", 8, h, max(l - 1, 0))
                    o = lev[l % 3]
                    ref = [cumv(c, L, L, 1).to_broadcast([P, LT, nb_, L]) for c in range(2)]
                    nc.gpsimd.tensor_tensor(halfv(o[:, 0], L, 0), ref[0], cumv(0, L, 1, L), ALU.subtract)
                    nc.gpsimd.tensor_tensor(halfv(o[:, 0], L, 1), cumv(1, L, L, L), ref[1], ALU.subtract)
                    nc.gpsimd.tensor_tensor(halfv(o[:, 1], L, 0), ref[1], cumv(1, L, 0, L), ALU.subtract)
                    nc.gpsimd.tensor_tensor(halfv(o[:, 1], L, 1), cumv(0, L, L + 1, L), ref[0], ALU.subtract).then_inc(z["x"], 1)
                    if l == 3:
                        W(pool, "o", 1, h, 0)
                        nc.gpsimd.tensor_tensor(kd[0][:], cum[0][:, :, P:P + 1].to_broadcast([P, NT, P]), cum[0][:, :, 1:P + 1], ALU.subtract).then_inc(z["kda"], 1)
                        nc.gpsimd.tensor_tensor(qi[1][:], cum[1][:, CT:NT, P:P + 1].to_broadcast([P, LT, P]), cum[1][:, CT:NT, 0:P], ALU.subtract).then_inc(z["qia"], 1)
                if after:
                    prologue(*after)

        @block.scalar
        def _(act):
            act.wait_ge(z["lam_steps"], 1)
            nc.scalar.activation(lb[:], gdiff[:], ACT.Sigmoid).then_inc(z["lam_steps"], 1)
            act.wait_ge(z["lam_steps"], 4)
            nc.scalar.activation(lame[:], lams[:], ACT.Exp).then_inc(z["lam_steps"], 1)

            def gates(hh, h, par):
                act.wait_ge(s_in[par], IN * hh + IN)
                W(act, "gate", 1, h, 0)
                nc.scalar.activation(sq[:], lat[par][:, HG_Q], ACT.Sigmoid).then_inc(z["sig"], 1)
                nc.scalar.activation(sg[:], lat[par][:, HG_G], ACT.Sigmoid).then_inc(z["sig"], 1)
                for d in range(2):
                    nc.scalar.activation(f[d][:, CTX:TOK], lat[par][:, HG_FF + d], ACT.Sigmoid).then_inc(z["sig"], 1)
                W(act, "tctx", 1, h, 1)
                for d in range(2):
                    nc.scalar.activation(f[d][:, 0:CTX], C[:, d * CTX:(d + 1) * CTX], ACT.Sigmoid).then_inc(z["sig"], 1)
                nc.scalar.activation(kt[:, 0:CTX], C[:, 2 * CTX:3 * CTX], ACT.Copy).then_inc(z["tctx_read"], 1)

            def tokens(hh, h, par):
                W(act, "tlat", 1, h, 1)
                nc.scalar.activation(iv[par][:], C[:].rearrange("p (a t n) -> p a t n", a=2, n=P), ACT.Copy).then_inc(z["tlat_read"], 1)

            def logs(hh, h, par):
                for d in range(2):
                    W(act, "f", 2, h, d + 1)
                    nc.scalar.activation(lf[d][:], f[d][:], ACT.Ln).then_inc(z["lf"], 1)

            gates(0, 0, 0)
            tokens(0, 0, 0)
            logs(0, 0, 0)
            for hh, h, par, after in heads(act):
                def exps(b):
                    for c, bank in enumerate((A, B)):
                        W(act, "nb", 8, h, 2 * b + c + 1)
                        if b >= 2:
                            W(act, "tp", 4, h, b - 1)
                        nc.scalar.activation(ex[c][b % 2][:], bank[:, 0:TOK], ACT.Exp, bias=nb[:, 2 * b + c:2 * b + c + 1],
                                             scale=0.125, accum_out=sums[:, 2 * b + c:2 * b + c + 1]).then_inc(z["e"], 1)

                def prob_t(b):
                    W(act, "tp", 4, h, b + 1)
                    if b >= 2:
                        W(act, "pv", 4, h, b - 1)
                    nc.scalar.activation(pt[b % 2][:], C[:, 0:TOK], ACT.Copy).then_inc(z["tp_read"], 1)

                def level(l):
                    W(act, "x", 7, h, l + 1)
                    nc.scalar.activation(lev[l % 3][:], lev[l % 3][:], ACT.Exp).then_inc(z["ex"], 1)

                exps(0)
                level(0)
                exps(1)
                level(1)
                prob_t(0)
                W(act, "cum", 2, h, 2)
                nc.scalar.activation(qi[0][:], cum[0][:, CT:NT, 1:P + 1], ACT.Exp).then_inc(z["qie"], 1)
                nc.scalar.activation(kd[1][:], cum[1][:, :, 0:P], ACT.Exp).then_inc(z["kde"], 1)
                for d in range(2):
                    nc.scalar.activation(dc[d][:], cum[d][:, :, P], ACT.Exp).then_inc(z["dc"], 1)
                exps(2)
                level(2)
                prob_t(1)
                level(3)
                exps(3)
                level(4)
                prob_t(2)
                W(act, "qia", 1, h, 1)
                nc.scalar.activation(qi[1][:], qi[1][:], ACT.Exp).then_inc(z["qie"], 1)
                W(act, "kda", 1, h, 1)
                nc.scalar.activation(kd[0][:], kd[0][:], ACT.Exp).then_inc(z["kde"], 1)
                level(5)
                prob_t(3)
                level(6)
                W(act, "pv", 4, h, 4)
                nc.scalar.activation(sqd[:], E[:], ACT.Square).then_inc(z["dsq"], 1)
                for d in range(2):
                    W(act, "tkd", 2, h, d + 1)
                    nc.scalar.activation(kdt[d][:], C[:, 0:TOK].rearrange("p (t n) -> p t n", n=P), ACT.Copy).then_inc(z["tkd_read"], 1)
                if after:
                    gates(*after)
                    tokens(*after)
                W(act, "o", 1, h, 1)
                nc.scalar.activation(sqh[:], F[:], ACT.Square).then_inc(z["hsq"], 1)
                W(act, "dss", 1, h, 1)
                nc.scalar.activation(rd[:], A[:, 0:SEQ], ACT.Ln, bias=k.eps[:], scale=1.0 / P).then_inc(z["dln"], 1)
                if after:
                    logs(*after)
                W(act, "hss", 1, h, 1)
                nc.scalar.activation(rh[:], B[:, 0:SEQ], ACT.Ln, bias=k.eps[:], scale=1.0 / P).then_inc(z["hln"], 1)
                W(act, "dln", 1, h, 1)
                nc.scalar.activation(rd[:], rd[:], ACT.Exp, scale=-0.5).then_inc(z["drs"], 1)
                W(act, "hln", 1, h, 1)
                nc.scalar.activation(rh[:], rh[:], ACT.Exp, scale=-0.5).then_inc(z["hrs"], 1)

        @block.vector
        def _(dve):
            v = nc.vector
            dve.sem_inc(z["done"], 2)
            dve.sem_inc(z["gate"], 1)
            dve.sem_inc(z["hmul"], 1)
            dve.wait_ge(z["const_in"], 128)
            v.tensor_copy(masks[:], mask_in)
            v.memset(cum[0][:, :, 0:1], 0.0)
            v.memset(cum[1][:, :, 0:1], 0.0)
            v.tensor_tensor(gdiff[:], gamma[:, 0], gamma[:, 1], ALU.subtract).then_inc(z["lam_steps"], 1)
            v.tensor_tensor(lamp[:], lamv[:, 0:2], lamv[:, 2:4], ALU.mult).then_inc(z["ready"], 1)
            dve.wait_ge(z["lam_steps"], 2)
            v.tensor_scalar(omlb[:], lb[:], -1.0, 1.0, ALU.mult, ALU.add).then_inc(z["lam_steps"], 1)
            dve.wait_ge(z["ready"], 1)
            v.tensor_reduce(lams[:], lamp[:], AX.X, ALU.add).then_inc(z["lam_steps"], 1)
            dve.wait_ge(z["lam_steps"], 5)
            v.tensor_tensor(neglam[:], lame[:, 1:2], lame[:, 0:1], ALU.subtract).then_inc(z["lam_steps"], 1)
            dve.wait_ge(z["lam_steps"], 6)
            v.tensor_scalar(neglam[:], neglam[:], -LAM_INIT, None, ALU.add).then_inc(z["lam_steps"], 1)
            v.tensor_scalar(dan[:], dan[:], 1.0 - LAM_INIT, None, ALU.mult).then_inc(z["lam_steps"], 1)
            dve.wait_ge(z["lam_steps"], 8)

            def forget(hh, h, par):
                W(dve, "sig", 6, h, 1)
                v.tensor_tensor(q[:], lat[par][:, HG_Q], sq[:], ALU.mult).then_inc(z["q"], 1)
                W(dve, "sig", 6, h, 6)
                for d in range(2):
                    col = bass.ds(h, 1)
                    v.tensor_scalar(f[d][:], f[d][:], omlb[:, d, col], lb[:, d, col], ALU.mult, ALU.add).then_inc(z["f_steps"], 1)
                    W(dve, "f_steps", 2, h, d + 1)
                    v.tensor_scalar(key[d][:], f[d][:], -1.0, 1.0, ALU.mult, ALU.add).then_inc(z["key"], 1)
                    W(dve, "key", 2, h, d + 1)
                    v.tensor_scalar(f[d][:], f[d][:], 2.0 ** -63, None, ALU.max).then_inc(z["f"], 1)

            def rotate_and_scan(hh, h, par):
                W(dve, "rot", 2, h, 2)
                v.tensor_tensor(ropet[:], C[:].rearrange("p (j n) -> p j n", j=2), sin[:].rearrange("p (o n) -> p o n", o=1).to_broadcast([P, 2, SEQ]),
                                ALU.mult).then_inc(z["rope_tmp"], 1)
                W(dve, "cos", 2, h, 2)
                W(dve, "rope_tmp", 1, h, 1)
                v.tensor_tensor(kt[:, CTX:TOK], kt[:, CTX:TOK], ropet[:, 0], ALU.add)
                v.tensor_tensor(qt[:], qt[:], ropet[:, 1], ALU.add).then_inc(z["kq"], 1)
                v.tensor_tensor(diag[:], key[0][:, CTX:TOK], key[1][:, CTX:TOK], ALU.add).then_inc(z["diag"], 1)
                for d in range(2):
                    W(dve, "lf", 2, h, d + 1)
                    for t in range(NT):
                        last = v.tensor_tensor_scan(cum[d][:, t, 1:P + 1], k.ones[:], lf[d][:, t * P:(t + 1) * P], 0.0, ALU.mult, ALU.add)
                    last.then_inc(z["cum"], 1)

            forget(0, 0, 0)
            rotate_and_scan(0, 0, 0)
            for hh, h, par, after in heads(dve):
                def maxima(b):
                    for c, bank in enumerate((A, B)):
                        col = slice(2 * b + c, 2 * b + c + 1)
                        W(dve, "s", 8, h, 2 * b + c + 1)
                        v.tensor_reduce(nmx[:, col], bank[:, 0:TOK], AX.X, ALU.max, negate=True).then_inc(z["mx"], 1)
                        W(dve, "mx", 8, h, 2 * b + c + 1)
                        v.tensor_scalar(nb[:, col], nmx[:, col], 0.125, None, ALU.mult).then_inc(z["nb"], 1)

                def probs(b):
                    W(dve, "e", 8, h, 2 * b + 2)
                    v.reciprocal(rinv[:, 2 * b:2 * b + 2], sums[:, 2 * b:2 * b + 2]).then_inc(z["inv"], 1)
                    W(dve, "inv", 8, h, 2 * b + 1)
                    v.tensor_tensor(rlam[:, b:b + 1], rinv[:, 2 * b + 1:2 * b + 2], neglam[:], ALU.mult).then_inc(z["inv"], 1)
                    W(dve, "inv", 8, h, 2 * b + 2)
                    v.tensor_scalar(ex[1][b % 2][:], ex[1][b % 2][:], rlam[:, b:b + 1], None, ALU.mult).then_inc(z["p_scaled"], 1)
                    W(dve, "p_scaled", 4, h, b + 1)
                    v.scalar_tensor_tensor(ex[0][b % 2][:], ex[0][b % 2][:], rinv[:, 2 * b:2 * b + 1], ex[1][b % 2][:], ALU.mult, ALU.add).then_inc(z["p"], 1)

                def operands(l):
                    L = P >> (l + 1)
                    o = lev[l % 3]
                    W(dve, "ex", 7, h, l + 1)
                    for j in range(2):
                        v.tensor_tensor(halfv(o[:, 0], L, j), halfv(o[:, 0], L, j), halfv(key[j][:, CTX:TOK], L, j), ALU.mult)
                    v.tensor_tensor(o[:, 1], o[:, 1], q[:], ALU.mult).then_inc(z["ab"], 1)

                def collect(l):
                    W(dve, "lv", 8, h, l + 1)
                    if l == 0:
                        v.tensor_copy(sc[:], F[:]).then_inc(z["sc"], 1)
                    else:
                        W(dve, "sc", 8, h, l)
                        dve.sem_inc(z["turn"], 1)
                        v.copy_predicated(sc[:].rearrange("p (t n) -> p t n", t=LT), masks[:, l - 1:l].to_broadcast([P, LT, P]),
                                          F[:].rearrange("p (t n) -> p t n", t=LT)).then_inc(z["sc"], 1)

                maxima(0)
                collect(0)
                maxima(1)
                operands(0)
                probs(0)
                collect(1)
                operands(1)
                probs(1)
                maxima(2)
                collect(2)
                operands(2)
                probs(2)
                maxima(3)
                collect(3)
                operands(3)
                probs(3)
                collect(4)
                operands(4)
                W(dve, "qie", 2, h, 2)
                for d in range(2):
                    last = v.tensor_tensor(qi[d][:], qi[d][:], q[:].rearrange("p (t n) -> p t n", t=LT), ALU.mult)
                last.then_inc(z["qi"], 1)
                W(dve, "kde", 2, h, 2)
                for d in range(2):
                    v.tensor_tensor(kd[d][:], kd[d][:], key[d][:].rearrange("p (t n) -> p t n", t=NT), ALU.mult).then_inc(z["kd"], 1)
                collect(5)
                operands(5)
                collect(6)
                operands(6)
                collect(7)
                v.scalar_tensor_tensor(gate[:], lat[par][:, HG_G], hgn[:, bass.ds(h, 1)], sg[:], ALU.mult, ALU.mult).then_inc(z["gate"], 1)
                W(dve, "u", 1, h, 1)
                W(dve, "dc", 2, h, 2)
                uf = [B[:, t * P:(t + 1) * P] for t in range(4)] + [A[:, 512:512 + P]]
                ub = [B[:, 512 + t * P:512 + (t + 1) * P] for t in range(4)] + [A[:, 512 + P:512 + 2 * P]]
                for j in range(5):
                    for d, u, t in ((0, uf[j], j), (1, ub[j], (1, 0, 5, 4, 3)[j])):
                        if j == 0:
                            last = v.tensor_copy(st[d][:, 0], u)
                        else:
                            last = v.scalar_tensor_tensor(st[d][:, j], st[d][:, j - 1], dc[d][:, t:t + 1], u, ALU.mult, ALU.add)
                    last.then_inc(z["state"], 1)
                    if j < 4:
                        W(dve, "state", 5, h, j + 1)
                if after:
                    forget(*after)
                    rotate_and_scan(*after)
                W(dve, "drs", 1, h, 1)
                v.scalar_tensor_tensor(k.mix[:, bass.ds(h + HEADS, 1)].rearrange("p a n -> p (a n)"), E[:], dan[:, bass.ds(h, 1)], rd[:], ALU.mult, ALU.mult).then_inc(z["hmul"], 1)
                W(dve, "hrs", 1, h, 1)
                v.tensor_tensor(hgo[:], F[:], rh[:], ALU.mult).then_inc(z["hmul"], 1)
                W(dve, "hmul", 2, h, 2)
                W(dve, "gate", 1, h, 1)
                v.tensor_tensor(k.mix[:, bass.ds(h, 1)].rearrange("p a n -> p (a n)"), hgo[:], gate[:], ALU.mult).then_inc(z["done"], 1)

        @block.tensor
        def _(pe):
            mm, tr = nc.tensor.matmul, nc.tensor.transpose
            pe.wait_ge(z["const_in"], 128)
            pe.sem_inc(z["lv"], 1)
            pe.sem_inc(z["o"], 1)
            pe.sem_inc(z["hln"], 1)
            pe.sem_inc(z["s"], 8)

            def context_transposed(hh, h, par):
                pe.wait_ge(s_in[par], IN * hh + IN)
                for j, part in enumerate((0, 1, 3)):
                    for t in range(CT):
                        last = tr(C[:, (j * CT + t) * P:(j * CT + t + 1) * P], cx[par][:, part, t], k.ident[:])
                last.then_inc(z["tctx"], 1)

            def latents_rotated(hh, h, par):
                W(pe, "tlat_read", 1, h, 1)
                mm(C[:, 0:SEQ], perm[:], lat[par][:, DA_K], start=True, stop=True).then_inc(z["rot"], 1)
                mm(C[:, SEQ:2 * SEQ], perm[:], lat[par][:, DA_Q], start=True, stop=True).then_inc(z["rot"], 1)

            def latents_transposed(hh, h, par):
                W(pe, "tctx_read", 1, h, 1)
                for j, part in enumerate((HG_I, DA_V)):
                    for t in range(LT):
                        last = tr(C[:, (j * LT + t) * P:(j * LT + t + 1) * P], lat[par][:, part, t * P:(t + 1) * P], k.ident[:])
                last.then_inc(z["tlat"], 1)

            context_transposed(0, 0, 0)
            latents_transposed(0, 0, 0)
            latents_rotated(0, 0, 0)
            for hh, h, par, after in heads(pe):
                def scores(b):
                    for c, bank in enumerate((A, B)):
                        if b >= 1:
                            W(pe, "e", 8, h, 2 * b + c - 1)
                        lanes = slice(64 * c, 64 * c + 64)
                        for lo, hi in ((0, 512), (512, TOK)):
                            last = mm(bank[:, lo:hi], qt[lanes, b * P:(b + 1) * P], kt[lanes, lo:hi], start=True, stop=True)
                        last.then_inc(z["s"], 1)

                def transpose_probs(b):
                    W(pe, "p", 4, h, b + 1)
                    if b == 0:
                        W(pe, "rope_tmp", 1, h, 1)
                    else:
                        W(pe, "tp_read", 4, h, b)
                    for t in range(NT):
                        last = tr(C[:, t * P:(t + 1) * P], ex[0][b % 2][:, t * P:(t + 1) * P], k.ident[:])
                    last.then_inc(z["tp"], 1)

                def attend(b):
                    W(pe, "tp_read", 4, h, b + 1)
                    for t in range(NT):
                        vt = cx[par][:, 4, t] if t < CT else iv[par][:, 1, t - CT]
                        last = mm(E[:, b * P:(b + 1) * P], vt, pt[b % 2][:, t * P:(t + 1) * P], start=t == 0, stop=t == NT - 1)
                    last.then_inc(z["pv"], 1)

                def level(l):
                    if l == 0:
                        W(pe, "diag", 1, h, 1)
                        W(pe, "q", 1, h, 1)
                        W(pe, "hmul", 2, h, 0)
                    else:
                        W(pe, "ab", 7, h, l)
                        W(pe, "sc", 8, h, l)
                    for t in range(LT):
                        w = slice(t * P, (t + 1) * P)
                        a, b_ = (diag[:, w], q[:, w]) if l == 0 else (lev[(l - 1) % 3][:, 0, w], lev[(l - 1) % 3][:, 1, w])
                        last = mm(F[:, w], a, b_, start=True, stop=True)
                    last.then_inc(z["lv"], 1)

                W(pe, "kq", 1, h, 1)
                W(pe, "tctx_read", 1, h, 1)
                W(pe, "hln", 1, h, 0)
                scores(0)
                level(0)
                scores(1)
                level(1)
                transpose_probs(0)
                scores(2)
                level(2)
                attend(0)
                transpose_probs(1)
                scores(3)
                level(3)
                attend(1)
                transpose_probs(2)
                level(4)
                attend(2)
                transpose_probs(3)
                level(5)
                attend(3)
                level(6)
                for d in range(2):
                    W(pe, "kd", 2, h, d + 1)
                    if d == 0:
                        W(pe, "tp_read", 4, h, 4)
                    else:
                        W(pe, "tkd_read", 2, h, 1)
                    for t in range(NT):
                        last = tr(C[:, t * P:(t + 1) * P], kd[d][:, t], k.ident[:])
                    last.then_inc(z["tkd"], 1)
                W(pe, "dsq", 1, h, 1)
                W(pe, "e", 8, h, 8)
                mm(A[:, 0:SEQ], k.ones[:], sqd[:], start=True, stop=True).then_inc(z["dss"], 1)
                level(7)
                W(pe, "tkd_read", 2, h, 2)
                if after:
                    context_transposed(*after)
                for j in range(5):
                    for d, t in ((0, j), (1, (1, 0, 5, 4, 3)[j])):
                        vt = cx[par][:, 2, t] if t < CT else iv[par][:, 0, t - CT]
                        out = B[:, d * 512 + j * P:d * 512 + (j + 1) * P] if j < 4 else A[:, 512 + d * P:512 + (d + 1) * P]
                        last = mm(out, kdt[d][:, t], vt, start=True, stop=True)
                last.then_inc(z["u"], 1)
                if after:
                    latents_transposed(*after)
                W(pe, "sc", 8, h, 8)
                W(pe, "qi", 1, h, 1)
                W(pe, "state", 5, h, 5)
                for t in range(LT):
                    w = slice(t * P, (t + 1) * P)
                    mm(F[:, w], iv[par][:, 0, t], sc[:, w], start=True, stop=False)
                    mm(F[:, w], st[0][:, t + 1], qi[0][:, t], start=False, stop=False)
                    last = mm(F[:, w], st[1][:, LT - t], qi[1][:, t], start=False, stop=True)
                last.then_inc(z["o"], 1)
                if after:
                    latents_rotated(*after)
                W(pe, "hsq", 1, h, 1)
                mm(B[:, 0:SEQ], k.ones[:], sqh[:], start=True, stop=True).then_inc(z["hss"], 1)


def output_and_query(nc, k, dram):
    with ExitStack() as ctx:
        sb = lambda n, s, d=F32: ctx.enter_context(nc.sbuf_tensor(n, s, d))
        pb = lambda n: ctx.enter_context(nc.psum_tensor(n, [P, 512], F32))
        sem = lambda n: k.semaphore(nc, n)
        stage = [sb(f"wo_stage{s}", [P, UNIT]) for s in range(2)]
        w_hi = [sb(f"wo_hi{s}", [P, UNIT // 2], F32R) for s in range(2)]
        w_lo = [sb(f"wo_lo{s}", [P, UNIT // 2], F32R) for s in range(2)]
        g2n, gain = sb("norm2_g", [P, KT]), sb("gain2", [P, KT])
        tmp = sb("x_delta", [P, 2, SEQ])
        xsq = sb("x1_sq", [P, 2, SEQ])
        rstd = sb("rstd2", [P, SEQ])
        p_out, p_ss = [pb(f"wo_out{s}") for s in range(4)], pb("ss2")
        names = "in mix_hi mix_lo hi lo mm ev x1 sq sqd ln rstd gain xn h h_hi h_lo "
        z = {n: sem("p3_" + n) for n in names.split()}
        s_w = [sem(f"p3_w_in{s}") for s in range(2)]
        block = ctx.enter_context(nc.Block())
        G = D // 512
        HALF = UNIT // 2

        @block.sync
        def _(sp):
            def load(w_name, first, g, u):
                sp.wait_ge(z["lo"], 8 * g + (8 * first + 2 * u + 1))
                sp.dma_start(stage[u % 2][:], dram[w_name][bass.ds(g, 1), :, u * UNIT:(u + 1) * UNIT].rearrange("a p n -> (a p) n")).then_inc(s_w[u % 2], 16)

            for u in range(4):
                load("w_out", 0, 0, u)
                if u == 1:
                    sp.dma_start(g2n[:], dram["norm2_g"]).then_inc(z["in"], 16)
            sp.dma_start(k.x[:], dram["x"]).then_inc(z["in"], 16)
            with sp.Fori(1, G) as g:
                for u in range(4):
                    load("w_out", 0, g, u)
            with sp.Fori(0, G) as g:
                for u in range(4):
                    load("w_query", G, g, u)

        @block.gpsimd
        def _(pool):
            pool.wait_ge(z["in"], 32)
            with pool.Fori(0, G) as g:
                for c in range(4):
                    tile = bass.ds(4 * g + c, 1)
                    pool.wait_ge(z["ev"], 4 * g + c + 5)
                    nc.gpsimd.tensor_tensor(k.x[:, tile].rearrange("p a n -> p (a n)"), k.x[:, tile].rearrange("p a n -> p (a n)"),
                                            tmp[:, c % 2], ALU.add).then_inc(z["x1"], 1)

        @block.scalar
        def _(act):
            act.sem_inc(z["ev"], 4)
            act.wait_ge(z["in"], 32)
            with act.Fori(0, G) as g:
                for c in range(4):
                    act.wait_ge(z["mm"], 32 * g + (28 + c + 1 + 8))
                    act.wait_ge(z["x1"], 4 * g + c + 1)
                    nc.scalar.activation(tmp[:, c % 2], p_out[c][:], ACT.Copy, scale=k.mod2[:, bass.ds(4 * g + c, 1)]).then_inc(z["ev"], 1)
                for c in range(4):
                    act.wait_ge(z["x1"], 4 * g + c + 3)
                    act.wait_ge(z["sqd"], 4 * g + c + 1)
                    nc.scalar.activation(xsq[:, c % 2], k.x[:, bass.ds(4 * g + c, 1)].rearrange("p a n -> p (a n)"), ACT.Square).then_inc(z["sq"], 1)
            act.wait_ge(z["sqd"], KT + 2)
            nc.scalar.activation(rstd[:], p_ss[:], ACT.Ln, bias=k.eps[:], scale=1.0 / D).then_inc(z["ln"], 1)
            act.wait_ge(z["ln"], 1)
            nc.scalar.activation(rstd[:], rstd[:], ACT.Exp, scale=-0.5).then_inc(z["rstd"], 1)
            act.wait_ge(z["gain"], 1)
            for t in range(KT):
                act.wait_ge(z["xn"], t + 1)
                nc.scalar.activation(k.q[:, t], k.q[:, t], ACT.Identity, bias=k.mod2[:, KT + t:KT + t + 1], scale=gain[:, t:t + 1]).then_inc(z["h"], 1)
            with act.Fori(G, 2 * G) as g:
                for c in range(4):
                    act.wait_ge(z["mm"], 32 * g + (28 + c + 1 + 8))
                    act.wait_ge(z["h_lo"], KT)
                    nc.scalar.activation(k.q[:, bass.ds(4 * g + (c - 4 * G), 1)].rearrange("p a n -> p (a n)"), p_out[c][:], ACT.Copy).then_inc(z["ev"], 1)

        @block.vector
        def _(dve):
            v = nc.vector
            dve.sem_inc(z["lo"], 3)

            def split(g, u, j, first):
                n = 8 * first + 2 * u + j
                dve.wait_ge(s_w[u % 2], 32 * g + (32 * first + 16 * (u // 2) + 16))
                dve.wait_ge(z["mm"], 32 * g + (4 * n + 4))
                w = slice(j * HALF, (j + 1) * HALF)
                v.tensor_copy(w_hi[j][:], stage[u % 2][:, w]).then_inc(z["hi"], 1)
                dve.wait_ge(z["hi"], 8 * g + (n + 1))
                v.tensor_tensor(w_lo[j][:], stage[u % 2][:, w], w_hi[j][:].bitcast(F32), ALU.subtract).then_inc(z["lo"], 1)

            for t in range(KT):
                v.tensor_copy(k.a_hi[:, t], k.mix[:, t]).then_inc(z["mix_hi"], 1)
                dve.wait_ge(z["mix_hi"], t + 1)
                v.tensor_tensor(k.a_lo[:, t], k.mix[:, t], k.a_hi[:, t].bitcast(F32), ALU.subtract).then_inc(z["mix_lo"], 1)
                if t == 0:
                    split(0, 0, 0, 0)
                    split(0, 0, 1, 0)
            for u in range(1, 4):
                for j in range(2):
                    split(0, u, j, 0)
            with dve.Fori(1, G) as g:
                for u in range(4):
                    for j in range(2):
                        split(g, u, j, 0)
            for j in range(2):
                split(0, 0, j, G)
            dve.wait_ge(z["in"], 32)
            v.scalar_tensor_tensor(gain[:], k.mod2[:, 2 * KT:3 * KT], 1.0, g2n[:], ALU.add, ALU.mult).then_inc(z["gain"], 1)
            dve.wait_ge(z["rstd"], 1)
            for t in range(KT):
                v.tensor_tensor(k.q[:, t], k.x[:, t], rstd[:], ALU.mult).then_inc(z["xn"], 1)
                if t >= 1:
                    dve.wait_ge(z["h"], t)
                    v.tensor_copy(k.a_hi[:, t - 1], k.q[:, t - 1]).then_inc(z["h_hi"], 1)
                    dve.wait_ge(z["h_hi"], t)
                    v.tensor_tensor(k.a_lo[:, t - 1], k.q[:, t - 1], k.a_hi[:, t - 1].bitcast(F32), ALU.subtract).then_inc(z["h_lo"], 1)
                if t % 2 == 0 and t >= 6:
                    split(0, (t // 2 - 1) // 2, (t // 2 - 1) % 2, G)
            dve.wait_ge(z["h"], KT)
            v.tensor_copy(k.a_hi[:, KT - 1], k.q[:, KT - 1]).then_inc(z["h_hi"], 1)
            dve.wait_ge(z["h_hi"], KT)
            v.tensor_tensor(k.a_lo[:, KT - 1], k.q[:, KT - 1], k.a_hi[:, KT - 1].bitcast(F32), ALU.subtract).then_inc(z["h_lo"], 1)
            split(0, 3, 1, G)
            with dve.Fori(1, G) as g:
                for u in range(4):
                    for j in range(2):
                        split(g, u, j, G)

        @block.tensor
        def _(pe):
            pe.sem_inc(z["mm"], 8)
            pe.sem_inc(z["sqd"], 2)
            pe.sem_inc(z["x1"], 2)

            def group(g, first, ready):
                for u in range(4):
                    for j in range(2):
                        pe.wait_ge(z["lo"], 8 * g + (8 * first + 2 * u + j + 4))
                        if ready is not None:
                            pe.wait_ge(z[ready], 4 * u + 2 * j + 2)
                        for c in range(4):
                            if u + j == 0:
                                pe.wait_ge(z["ev"], 4 * g + (4 * first + c + 1))
                            for t in range(2):
                                w, kt = slice(t * 512 + c * P, t * 512 + (c + 1) * P), 4 * u + 2 * j + t
                                nc.tensor.matmul(p_out[c][:], w_hi[j][:, w], k.a_hi[:, kt], start=kt == 0, stop=False)
                                nc.tensor.matmul(p_out[c][:], w_hi[j][:, w], k.a_lo[:, kt], start=False, stop=False)
                                last = nc.tensor.matmul(p_out[c][:], w_lo[j][:, w], k.a_hi[:, kt], start=False, stop=kt == KT - 1)
                            last.then_inc(z["mm"], 1)

            def sums(g, start, stop):
                for c in range(4):
                    pe.wait_ge(z["sq"], 4 * g + c + 1)
                    nc.tensor.matmul(p_ss[:], k.ones[:], xsq[:, c % 2], start=start and c == 0, stop=stop and c == 3).then_inc(z["sqd"], 1)

            group(0, 0, "mix_lo")
            group(1, 0, None)
            sums(0, True, False)
            with pe.Fori(2, G) as g:
                group(g, 0, None)
                sums(g - 1, False, False)
            sums(G - 1, False, True)
            group(0, G, "h_lo")
            with pe.Fori(1, G) as g:
                group(g, G, None)


def u_half(dram, i, j):
    return dram["u"][bass.ds(2 * i + j // 2, 1), :, (j % 2) * HT:(j % 2 + 1) * HT].rearrange("a p n -> (a p) n")


def multiply_u_half(nc, k, bank, u_hi, u_lo, j):
    for t in range(KT // 2):
        w, kt = slice(t * P, (t + 1) * P), (j % 2) * (KT // 2) + t
        nc.tensor.matmul(bank[:], u_hi[:, w], k.a_hi[:, kt], start=kt == 0, stop=False)
        nc.tensor.matmul(bank[:], u_hi[:, w], k.a_lo[:, kt], start=False, stop=False)
        last = nc.tensor.matmul(bank[:], u_lo[:, w], k.a_hi[:, kt], start=False, stop=kt == KT - 1)
    return last


def retrieval(nc, k, dram):
    with ExitStack() as ctx:
        sb = lambda n, s, d=F32: ctx.enter_context(nc.sbuf_tensor(n, s, d))
        sem = lambda n: k.semaphore(nc, n)
        HJ = 2 * HEADS
        keys = sb("sub_keys", [P, HJ, NKEYS])
        s_sb = [sb(f"key_scores{s}", [P, HJ, NKEYS]) for s in range(2)]
        sv, si, sif = sb("key_best", [P, HJ, TOPK]), sb("key_index", [P, HJ, TOPK], U32), sb("key_index_f", [P, HJ, TOPK])
        best, ci = sb("best", [P, HEADS, TOPK]), sb("best_index", [P, HEADS, TOPK], U32)
        cab, cabf = sb("pair_index", [P, 2, HEADS * TOPK], U32), sb("pair_index_f", [P, 2, HEADS * TOPK])
        iota16 = sb("iota16", [P, TOPK])
        pick1 = sb("pick1", [P, HEADS * TOPK, TOPK])
        as_cand = lambda s: s_sb[s][:].rearrange("p j n -> p (j n)").rearrange("p (h n) -> p h n", h=HEADS)
        as_hot = lambda s: (s_sb[s][:].rearrange("p j n -> p (j n)").rearrange("p (n a) -> p n a", a=TOPK), pick1[:])
        u_st = [sb(f"pre_u_stage{s}", [P, HT]) for s in range(2)]
        u_hi, u_lo = ([sb(f"pre_u_{n}{s}", [P, HT], F32R) for s in range(2)] for n in ("hi", "lo"))
        af = [sb(f"pre_act{s}", [P, SEQ]) for s in range(2)]
        pu = [ctx.enter_context(nc.psum_tensor(f"p_pre_u{s}", [P, 512], F32)) for s in range(2)]
        res = sb("picked", [P, 3, HEADS * TOPK])
        gsum, ginv = sb("softmax_sum", [P, HEADS]), sb("softmax_inv", [P, HEADS])
        ps = [ctx.enter_context(nc.psum_tensor(f"p_scores{s}", [P, HJ * NKEYS // 2], F32)) for s in range(2)]
        pt = ctx.enter_context(nc.psum_tensor("p_picked", [P, 512], F32))
        names = ("turn in s ev m1 i1 r1 m2 i2 sif cand cm1 ci1 cr1 cm2 ci2 ab abf eq pick red gd ge gs gi g tr tread "
                 "u_hi u_lo umm act")
        z = {n: sem("p4_" + n) for n in names.split()}
        s_u, s_st = ([sem(f"p4_{n}{s}") for s in range(2)] for n in ("u_in", "act_stored"))
        block = ctx.enter_context(nc.Block())
        LOW = -3.0e38

        @block.sync
        def _(sp):
            sp.dma_start(keys[:], dram["sub_keys"]).then_inc(z["in"], 16)
            sp.dma_start(iota16[:], dram["iota"][:, 0:TOPK]).then_inc(z["in"], 16)

            def load(i, j):
                sp.wait_ge(z["u_lo"], 4 * i + (j + 1))
                sp.dma_start(u_st[j % 2][:], u_half(dram, i, j)).then_inc(s_u[j % 2], 16)

            def store(i, a):
                sp.wait_ge(z["act"], 2 * i + (a + 3))
                sp.dma_start(dram["act"][bass.ds(2 * i + a, 1)].rearrange("a p n -> (a p) n"), af[a][:]).then_inc(s_st[a], 16)

            for j in range(4):
                load(0, j)
            with sp.Fori(0, EARLY - 1) as i:
                load(i + 1, 0)
                load(i + 1, 1)
                store(i, 0)
                load(i + 1, 2)
                load(i + 1, 3)
                store(i, 1)
            for a in range(2):
                store(EARLY - 1, a)
            for a in range(2):
                sp.wait_ge(s_st[a], 16 * (EARLY + 1))

        @block.gpsimd
        def _(pool):
            pool.sem_inc(z["u_lo"], 2)
            with pool.Fori(0, EARLY) as i:
                for j in range(4):
                    pool.wait_ge(z["u_hi"], 4 * i + (j + 1))
                    nc.gpsimd.tensor_tensor(u_lo[j % 2][:], u_st[j % 2][:], u_hi[j % 2][:].bitcast(F32), ALU.subtract).then_inc(z["u_lo"], 1)

        @block.tensor
        def _(pe):
            pe.wait_ge(z["in"], 32)

            def scores(t):
                for j in range(HJ):
                    half, col = j // HEADS, j % HEADS
                    if col == 0 and t > 0:
                        pe.wait_ge(z["ev"], 2 * t - 1 + half)
                    last = nc.tensor.matmul(ps[half][:, col * NKEYS:(col + 1) * NKEYS], k.q[:, j, t * P:(t + 1) * P],
                                            keys[:, j], start=True, stop=True)
                    if col == HEADS - 1:
                        last.then_inc(z["s"], 1)

            pe.sem_inc(z["tr"], 1)
            pe.sem_inc(z["umm"], 2)
            scores(0)
            for t in range(LT):
                if t + 1 < LT:
                    scores(t + 1)
                with pe.Fori(sum(EARLY_OF[:t]), sum(EARLY_OF[:t + 1])) as i:
                    for j in range(4):
                        a = j // 2
                        pe.wait_ge(z["u_lo"], 4 * i + (j + 3))
                        if j % 2 == 0:
                            pe.wait_ge(z["act"], 2 * i + (a + 1))
                        multiply_u_half(nc, k, pu[a], u_hi[j % 2], u_lo[j % 2], j).then_inc(z["umm"], 1)
                pe.wait_ge(z["red"], 2 * t + 2)
                pe.wait_ge(z["g"], t + 1)
                if t > 0:
                    pe.wait_ge(z["tread"], t)
                for j in range(3):
                    last = nc.tensor.transpose(pt[:, j * P:(j + 1) * P], res[:, j], k.ident[:])
                last.then_inc(z["tr"], 1)

        @block.scalar
        def _(act):
            def evacuate(t, s):
                if t >= 2:
                    act.wait_ge(z["red"], 2 * (t - 1))
                for half in range(2):
                    act.wait_ge(z["s"], 2 * t + (half + 1))
                    nc.scalar.activation(s_sb[s][:, half * HEADS:(half + 1) * HEADS], ps[half][:].rearrange("p (a n) -> p a n", n=NKEYS),
                                         ACT.Copy).then_inc(z["ev"], 1)

            def high(i, j):
                act.wait_ge(s_u[j % 2], 32 * i + 16 * (j // 2) + 16)
                act.wait_ge(z["umm"], 4 * i + (j + 1))
                nc.scalar.activation(u_hi[j % 2][:], u_st[j % 2][:], ACT.Copy).then_inc(z["u_hi"], 1)

            def gelu(i, a):
                act.wait_ge(z["umm"], 4 * i + (2 * a + 4))
                act.wait_ge(s_st[a], 16 * i + 16)
                nc.scalar.activation(af[a][:], pu[a][:], ACT.Gelu).then_inc(z["act"], 1)

            def pair(i, more):
                high(i, 2)
                high(i, 3)
                gelu(i, 0)
                if more:
                    high(i + 1, 0)
                    high(i + 1, 1)
                gelu(i, 1)

            act.sem_inc(z["act"], 2)
            act.sem_inc(s_st[0], 16)
            act.sem_inc(s_st[1], 16)
            high(0, 0)
            high(0, 1)
            evacuate(0, 0)
            evacuate(1, 1)
            for t in range(LT):
                last_tile = t == LT - 1
                with act.Fori(sum(EARLY_OF[:t]), sum(EARLY_OF[:t + 1]) - last_tile) as i:
                    pair(i, True)
                if last_tile:
                    pair(EARLY - 1, False)
                act.wait_ge(z["gd"], t + 1)
                nc.scalar.activation(res[:, 2], res[:, 2], ACT.Exp).then_inc(z["ge"], 1)
                act.wait_ge(z["tr"], t + 2)
                nc.scalar.activation(k.picked[:, :, bass.ds(t * P, P)], pt[:, 0:3 * P].rearrange("p (j n) -> p j n", j=3), ACT.Copy).then_inc(z["tread"], 1)
                if t + 2 < LT:
                    evacuate(t + 2, t % 2)

        @block.vector
        def _(dve):
            v = nc.vector
            dve.wait_ge(z["in"], 32)

            def top16(t, tag, n, src, val, idx):
                for j in range(n):
                    last = v.max(val(j)[:, 0:8], src(j))
                last.then_inc(z[tag + "m1"], 1)
                dve.wait_ge(z[tag + "m1"], t + 1)
                dve.sem_inc(z["turn"], 1)
                for j in range(n):
                    last = v.max_index(idx(j)[:, 0:8], val(j)[:, 0:8], src(j))
                last.then_inc(z[tag + "i1"], 1)
                dve.wait_ge(z[tag + "i1"], t + 1)
                dve.sem_inc(z["turn"], 1)
                for j in range(n):
                    last = v.match_replace(src(j), val(j)[:, 0:8], src(j), LOW)
                last.then_inc(z[tag + "r1"], 1)
                dve.wait_ge(z[tag + "r1"], t + 1)
                dve.sem_inc(z["turn"], 1)
                for j in range(n):
                    last = v.max(val(j)[:, 8:16], src(j))
                last.then_inc(z[tag + "m2"], 1)
                dve.wait_ge(z[tag + "m2"], t + 1)
                dve.sem_inc(z["turn"], 1)
                for j in range(n):
                    last = v.max_index(idx(j)[:, 8:16], val(j)[:, 8:16], src(j))
                last.then_inc(z[tag + "i2"], 1)
                dve.wait_ge(z[tag + "i2"], t + 1)
                dve.sem_inc(z["turn"], 1)

            def finish(t):
                w = res[:, 2].rearrange("p (h n) -> p h n", n=TOPK)
                dve.wait_ge(z["ge"], t + 1)
                v.tensor_reduce(gsum[:], w, AX.X, ALU.add).then_inc(z["gs"], 1)
                dve.wait_ge(z["gs"], t + 1)
                v.reciprocal(ginv[:], gsum[:]).then_inc(z["gi"], 1)
                dve.wait_ge(z["gi"], t + 1)
                v.tensor_tensor(w, w, ginv[:].rearrange("p (h o) -> p h o", o=1).to_broadcast([P, HEADS, TOPK]), ALU.mult).then_inc(z["g"], 1)

            for t in range(LT):
                s, before = t % 2, t - 1 if t else None
                dve.wait_ge(z["ev"], 2 * t + 2)
                dve.sem_inc(z["turn"], 1)
                top16(t, "", HJ, lambda j: s_sb[s][:, j], lambda j: sv[:, j], lambda j: si[:, j])
                if before is not None:
                    finish(before)
                v.tensor_copy(sif[:], si[:]).then_inc(z["sif"], 1)
                pair = sv[:].rearrange("p (h j) a -> p h j a", j=2)
                shape = [P, HEADS, TOPK, TOPK]
                cand, hot = as_cand(s), as_hot(s)
                v.tensor_tensor(cand.rearrange("p h (a b) -> p h a b", a=TOPK),
                                pair[:, :, 0, :].rearrange("p h (a o) -> p h a o", o=1).to_broadcast(shape),
                                pair[:, :, 1, :].rearrange("p h (o b) -> p h o b", o=1).to_broadcast(shape), ALU.add).then_inc(z["cand"], 1)
                dve.wait_ge(z["cand"], t + 1)
                dve.sem_inc(z["turn"], 1)
                top16(t, "c", HEADS, lambda h: cand[:, h], lambda h: best[:, h], lambda h: ci[:, h])
                flat = ci[:].rearrange("p h n -> p (h n)")
                v.tensor_single_scalar(cab[:, 0], flat, 4, ALU.logical_shift_right)
                v.tensor_single_scalar(cab[:, 1], flat, 15, ALU.bitwise_and).then_inc(z["ab"], 1)
                dve.wait_ge(z["tr"], t + 1)
                v.tensor_tensor(res[:, 2].rearrange("p (h n) -> p h n", n=TOPK), best[:], best[:, :, 0:1].to_broadcast([P, HEADS, TOPK]),
                                ALU.subtract).then_inc(z["gd"], 1)
                dve.wait_ge(z["ab"], t + 1)
                v.tensor_copy(cabf[:], cab[:]).then_inc(z["abf"], 1)
                dve.wait_ge(z["abf"], t + 1)
                shape = [P, HEADS * TOPK, TOPK]
                for j in range(2):
                    v.tensor_tensor(hot[j], cabf[:, j].rearrange("p (n o) -> p n o", o=1).to_broadcast(shape),
                                    iota16[:].rearrange("p (o a) -> p o a", o=1).to_broadcast(shape), ALU.is_equal).then_inc(z["eq"], 1)
                for j in range(2):
                    dve.wait_ge(z["eq"], 2 * t + (j + 1))
                    by_head = hot[j].rearrange("p (h n) a -> p h n a", n=TOPK)
                    index = sif[:].rearrange("p (h j) (o a) -> p h j o a", j=2, o=1)[:, :, j]
                    v.tensor_tensor(by_head, by_head, index.to_broadcast([P, HEADS, TOPK, TOPK]), ALU.mult).then_inc(z["pick"], 1)
                for j in range(2):
                    dve.wait_ge(z["pick"], 2 * t + (j + 1))
                    v.tensor_reduce(res[:, j], hot[j], AX.X, ALU.add).then_inc(z["red"], 1)
            finish(LT - 1)


def float_buffers(k):
    free = k.q[:].rearrange("p k n -> p (k n)")
    cut = lambda start, n: [free[:, start + s * n:start + (s + 1) * n] for s in range(2)]
    return cut(4 * HT, HT), cut(0, HT), cut(6 * HT, SEQ), cut(7 * HT, SEQ)


def v_half(dram, i, j):
    return dram["v"][bass.ds(2 * i + j % 2, 1), :, (j // 2) * HT:(j // 2 + 1) * HT].rearrange("a p n -> (a p) n")


def gate_matrix(nc, k, dram):
    with ExitStack() as ctx:
        sb = lambda n, s, d=F32: ctx.enter_context(nc.sbuf_tensor(n, s, d))
        sem = lambda n: k.semaphore(nc, n)
        QUAD = 4
        iota = sb("iota128", [P, NKEYS])
        hots = k.q[:].rearrange("p k n -> p (k n)")[:, 0:8 * QUAD * NKEYS].rearrange("p (s n a) -> p s n a", n=QUAD, a=NKEYS)
        hot1, hot2 = hots[:, 0:4], hots[:, 4:8]
        u_st, _, _, af = float_buffers(k)
        k.u_in, k.act_in = ([sem(f"p6_{n}_in{s}") for s in range(2)] for n in ("u", "act"))
        gs = [sb(f"gate_block{s}", [P, NKEYS, TB]) for s in range(2)]
        pg = [ctx.enter_context(nc.psum_tensor(f"p_gate{s}", [P, 512], F32)) for s in range(4)]
        z = {n: sem("p5_" + n) for n in ("in", "hot1", "diff2", "hot2", "mm", "ev")}
        s_st = k.gates_stored = [sem(f"p5_stored{s}") for s in range(2)]
        block = ctx.enter_context(nc.Block())
        QB = TB // QUAD
        k.all_gates_stored = 16 * (SEQ // TB // 2 + 1)

        @block.sync
        def _(sp):
            sp.dma_start(iota[:], dram["iota"]).then_inc(z["in"], 16)
            for s in range(2):
                sp.dma_start(u_st[s], u_half(dram, EARLY, s)).then_inc(k.u_in[s], 16)
                sp.dma_start(af[s], dram["act"][s]).then_inc(k.act_in[s], 16)
            with sp.Fori(0, SEQ // TB // 2) as b:
                for s in range(2):
                    sp.wait_ge(z["ev"], 2 * QB * b + (QB * (s + 1) + 4))
                    sp.dma_start(dram["gate"][:, bass.ds(2 * b + s, 1)].rearrange("p o a n -> p (o a) n"), gs[s][:]).then_inc(s_st[s], 16)
        @block.vector
        def _(dve):
            dve.wait_ge(z["in"], 16)
            with dve.Fori(0, SEQ // 16) as i:
                for s in range(4):
                    dve.wait_ge(z["mm"], 4 * i + s + 1)
                    for n in range(QUAD):
                        tok = bass.ds(16 * i + (4 * s + n), 1)
                        last = nc.vector.tensor_scalar(hot1[:, s, n], iota[:], k.picked[:, 0, tok], k.picked[:, 2, tok], ALU.is_equal, ALU.mult)
                    last.then_inc(z["hot1"], 1)
                    dve.wait_ge(z["diff2"], 4 * i + s + 1)
                    nc.vector.tensor_scalar(hot2[:, s], hot2[:, s], 0.0, None, ALU.is_equal).then_inc(z["hot2"], 1)

        @block.gpsimd
        def _(pool):
            pool.wait_ge(z["in"], 16)
            with pool.Fori(0, SEQ // 16) as i:
                for s in range(4):
                    pool.wait_ge(z["mm"], 4 * i + s + 1)
                    second = k.picked[:, 1, bass.ds(16 * i + 4 * s, QUAD)].rearrange("p (n o) -> p n o", o=1)
                    nc.gpsimd.tensor_tensor(hot2[:, s], second.to_broadcast([P, QUAD, NKEYS]),
                                            iota[:].rearrange("p (o a) -> p o a", o=1).to_broadcast([P, QUAD, NKEYS]),
                                            ALU.subtract).then_inc(z["diff2"], 1)

        @block.tensor
        def _(pe):
            pe.sem_inc(z["mm"], 4)
            with pe.Fori(0, SEQ // 16) as i:
                for s in range(4):
                    pe.wait_ge(z["hot1"], 4 * i + s + 1)
                    pe.wait_ge(z["hot2"], 4 * i + s + 1)
                    pe.wait_ge(z["ev"], 4 * i + s + 1)
                    for n in range(QUAD):
                        last = nc.tensor.matmul(pg[s][:, n * NKEYS:(n + 1) * NKEYS], hot2[:, s, n], hot1[:, s, n], start=True, stop=True)
                    last.then_inc(z["mm"], 1)

        @block.scalar
        def _(act):
            act.sem_inc(z["ev"], 4)
            act.sem_inc(s_st[0], 16)
            act.sem_inc(s_st[1], 16)
            with act.Fori(0, SEQ // TB // 2) as b:
                for r in range(2):
                    act.wait_ge(s_st[r], 16 * b + 16)
                    with act.Fori(0, QB // 4) as i:
                        for s in range(4):
                            act.wait_ge(z["mm"], 2 * QB * b + (QB * r + s + 5) + 4 * i)
                            out = gs[r][:, :, bass.ds(16 * i + 4 * s, QUAD)].rearrange("p a n -> p n a")
                            nc.scalar.activation(out, pg[s][:].rearrange("p (n a) -> p n a", n=QUAD), ACT.Copy).then_inc(z["ev"], 1)


def experts(nc, k, dram):
    with ExitStack() as ctx:
        sb = lambda n, s, d=F32: ctx.enter_context(nc.sbuf_tensor(n, s, d))
        pb = lambda n: ctx.enter_context(nc.psum_tensor(n, [P, 512], F32))
        sem = lambda n: k.semaphore(nc, n)
        u_st, v_st, gt, af = float_buffers(k)
        u_hi, u_lo = [sb(f"u_hi{s}", [P, HT], F32R) for s in range(4)], [sb(f"u_lo{s}", [P, HT], F32R) for s in range(4)]
        v_hi, v_lo = [sb(f"v_hi{s}", [P, HT], F32R) for s in range(4)], [sb(f"v_lo{s}", [P, HT], F32R) for s in range(4)]
        a_hi, a_lo = ([[sb(f"act_{n}{q}", [P, SEQ], F32R), second] for q in range(2)] for n in ("hi", "lo")
                      for second in [sb(f"act_{n}_second", [P, SEQ], F32R)])
        pu, pv = [pb(f"p_u{s}") for s in range(2)], [pb(f"p_v{s}") for s in range(6)]
        names = "u_hi u_lo v_hi v_lo umm vmm act ga ahi alo ev"
        z = {n: sem("p6_" + n) for n in names.split()}
        s_v, s_g = ([sem(f"p6_{n}_in{s}") for s in range(2)] for n in ("v", "gates"))
        s_u, s_af = k.u_in, k.act_in
        block = ctx.enter_context(nc.Block())
        N = E_TILES // PAIR

        def pairs(eng):
            with eng.Fori(0, (EARLY - 1) // 2) as h:
                for q in range(2):
                    yield 2 * h + q, q, True, "early"
            yield EARLY - 1, 0, True, None
            with eng.Fori(EARLY, N - 1) as i:
                yield i, 0, False, "u"
            yield N - 1, 0, False, None

        @block.sync
        def _(sp):
            def load_u(i, j):
                sp.wait_ge(z["u_lo"], 4 * i + (j + 1))
                sp.dma_start(u_st[j % 2], u_half(dram, i, j)).then_inc(s_u[j % 2], 16)

            def load_v(i, j):
                sp.wait_ge(z["v_lo"], 4 * i + (j + 1))
                sp.dma_start(v_st[j % 2], v_half(dram, i, j)).then_inc(s_v[j % 2], 16)

            def load_act(i, a):
                sp.wait_ge(z["alo"], 2 * i + (a + 1))
                sp.dma_start(af[a], dram["act"][bass.ds(2 * i + a, 1)].rearrange("a p n -> (a p) n")).then_inc(s_af[a], 16)

            def load_gates(i, a):
                sp.wait_ge(z["ga"], 2 * i + (a + 1))
                sp.dma_start(gt[a].rearrange("p (b n) -> p b n", n=TB), dram["gate"][:, :, bass.ds(2 * i + a, 1)].rearrange("p b o n -> p b (o n)")).then_inc(s_g[a], 16)

            load_v(0, 0)
            load_v(0, 1)
            load_u(EARLY, 2)
            load_u(EARLY, 3)
            for s in range(2):
                sp.wait_ge(k.gates_stored[s], k.all_gates_stored)
            load_gates(0, 0)
            load_gates(0, 1)
            load_v(0, 2)
            load_v(0, 3)
            with sp.Fori(1, EARLY) as i:
                for j in range(4):
                    load_v(i, j)
                    if j < 2:
                        load_act(i, j)
                        load_gates(i, j)
            with sp.Fori(EARLY, N - 1) as i:
                for j in range(4):
                    load_v(i, j)
                    if j < 2:
                        load_gates(i, j)
                for j in range(4):
                    load_u(i + 1, j)
            for j in range(4):
                load_v(N - 1, j)
                if j < 2:
                    load_gates(N - 1, j)

        @block.scalar
        def _(act):
            def u_high(i, j):
                act.wait_ge(s_u[j % 2], 32 * i + 16 * (j // 2) + 16)
                act.wait_ge(z["umm"], 4 * i + (j + 1))
                nc.scalar.activation(u_hi[j][:], u_st[j % 2], ACT.Copy).then_inc(z["u_hi"], 1)

            def v_high(i, j):
                act.wait_ge(s_v[j % 2], 32 * i + 16 * (j // 2) + 16)
                act.wait_ge(z["vmm"], 16 * i + (8 * (j // 2) + 8))
                nc.scalar.activation(v_hi[j][:], v_st[j % 2], ACT.Copy).then_inc(z["v_hi"], 1)

            def gelu(i, a):
                act.wait_ge(z["umm"], 4 * i + (2 * a + 6))
                act.wait_ge(z["alo"], 2 * i + (a + 1))
                nc.scalar.activation(af[a], pu[a][:], ACT.Gelu).then_inc(z["act"], 1)

            act.sem_inc(z["act"], 2 + 2 * EARLY)
            act.sem_inc(z["u_hi"], 4 * EARLY)
            for s in range(2):
                act.sem_inc(s_u[s], 32 * EARLY)
            act.wait_ge(k.gates_stored[0], k.all_gates_stored)
            for j in range(4):
                u_high(EARLY, j)
            act.wait_ge(k.gates_stored[1], k.all_gates_stored)
            for i, _, early, prepare in pairs(act):
                v_high(i, 0)
                v_high(i, 1)
                if not early:
                    gelu(i, 0)
                v_high(i, 2)
                v_high(i, 3)
                if not early:
                    gelu(i, 1)
                for j in range(4 if prepare == "u" else 0):
                    u_high(i + 1, j)

        @block.vector
        def _(dve):
            v = nc.vector
            dve.sem_inc(z["v_lo"], 2)
            dve.sem_inc(z["ga"], 2)
            dve.sem_inc(z["alo"], 2)
            dve.sem_inc(z["ev"], 4)

            dve.sem_inc(z["u_lo"], 2 + 4 * EARLY)

            def u_low(i, j):
                dve.wait_ge(z["u_hi"], 4 * i + (j + 1))
                v.tensor_tensor(u_lo[j][:], u_st[j % 2], u_hi[j][:].bitcast(F32), ALU.subtract).then_inc(z["u_lo"], 1)

            def v_low(i, j):
                dve.wait_ge(z["v_hi"], 4 * i + (j + 1))
                v.tensor_tensor(v_lo[j][:], v_st[j % 2], v_hi[j][:].bitcast(F32), ALU.subtract).then_inc(z["v_lo"], 1)

            def weigh(i, q, a, early):
                if early:
                    dve.wait_ge(s_af[a], 16 * i + 16)
                else:
                    dve.wait_ge(z["act"], 2 * i + (a + 3))
                    dve.wait_ge(z["vmm"], 16 * i + 16)
                dve.wait_ge(s_g[a], 16 * i + 16)
                v.tensor_tensor(af[a], af[a], gt[a], ALU.mult).then_inc(z["ga"], 1)
                dve.wait_ge(z["ga"], 2 * i + (a + 3))
                v.tensor_copy(a_hi[q][a][:], af[a]).then_inc(z["ahi"], 1)
                dve.wait_ge(z["ahi"], 2 * i + (a + 1))
                v.tensor_tensor(a_lo[q][a][:], af[a], a_hi[q][a][:].bitcast(F32), ALU.subtract).then_inc(z["alo"], 1)

            def operands(i, q, early):
                v_low(i, 0)
                v_low(i, 1)
                weigh(i, q, 0, early)
                v_low(i, 2)
                v_low(i, 3)
                weigh(i, q, 1, early)

            for j in range(4):
                u_low(EARLY, j)
            operands(0, 0, True)
            for i, q, early, prepare in pairs(dve):
                if not early:
                    operands(i, q, False)
                for m in range(KT):
                    dve.wait_ge(z["vmm"], 16 * i + (m + 17))
                    v.scalar_tensor_tensor(k.x[:, m], pv[m % 6][:], k.mod2[:, 3 * KT + m:3 * KT + m + 1], k.x[:, m], ALU.mult, ALU.add).then_inc(z["ev"], 1)
                    if m % 4 == 1 and prepare == "u":
                        u_low(i + 1, m // 4)
                    if prepare == "early" and m in (9, 11):
                        v_low(i + 1, m // 2 - 4)
                    if prepare == "early" and m == 13:
                        weigh(i + 1, 1 - q, 0, True)
                if prepare == "early":
                    weigh(i + 1, 1 - q, 1, True)
                    v_low(i + 1, 2)
                    v_low(i + 1, 3)

        @block.tensor
        def _(pe):
            pe.sem_inc(z["umm"], 4 + 4 * EARLY)
            pe.sem_inc(z["vmm"], 16)

            def multiply_u(i):
                for j in range(4):
                    a = j // 2
                    pe.wait_ge(z["u_lo"], 4 * i + (j + 3))
                    if j % 2 == 0:
                        pe.wait_ge(z["act"], 2 * i + (a + 1))
                    multiply_u_half(nc, k, pu[a], u_hi[j], u_lo[j], j).then_inc(z["umm"], 1)

            def multiply_v(i, q):
                first = [(m, a) for a in range(PAIR) for m in range(6)]
                for m, a in first + [(m, a) for m in range(6, KT) for a in range(PAIR)]:
                    j = 2 * (m // 8) + a
                    w = slice(m % 8 * P, (m % 8 + 1) * P)
                    if m % 8 == 0:
                        pe.wait_ge(z["v_lo"], 4 * i + (j + 3))
                    if m == 0:
                        pe.wait_ge(z["alo"], 2 * i + (a + 3))
                    if a == 0 and m < 4:
                        pe.wait_ge(z["ev"], 16 * i + (m + 1))
                    if a == 0 and m >= 6:
                        pe.wait_ge(z["ev"], 16 * i + (m - 1))
                    nc.tensor.matmul(pv[m % 6][:], v_hi[j][:, w], a_hi[q][a][:], start=a == 0, stop=False)
                    nc.tensor.matmul(pv[m % 6][:], v_hi[j][:, w], a_lo[q][a][:], start=False, stop=False)
                    last = nc.tensor.matmul(pv[m % 6][:], v_lo[j][:, w], a_hi[q][a][:], start=False, stop=a == PAIR - 1)
                    if a == PAIR - 1:
                        last.then_inc(z["vmm"], 1)

            multiply_u(EARLY)
            for i, q, early, prepare in pairs(pe):
                multiply_v(i, q)
                if prepare == "u":
                    multiply_u(i + 1)


def final_norm(nc, k, dram):
    with ExitStack() as ctx:
        sb = lambda n, s, d=F32: ctx.enter_context(nc.sbuf_tensor(n, s, d))
        sem = lambda n: k.semaphore(nc, n)
        fg, rstd, xsq = sb("final_g", [P, KT]), sb("rstd3", [P, SEQ]), sb("x2_sq", [P, KT, SEQ])
        ss = ctx.enter_context(nc.psum_tensor("ss3", [P, SEQ], F32))
        z = {n: sem("p7_" + n) for n in ("in", "sq", "ss", "ln", "rstd", "y", "st")}
        block = ctx.enter_context(nc.Block())

        @block.sync
        def _(sp):
            sp.dma_start(fg[:], dram["final_norm_g"]).then_inc(z["in"], 16)
            for q in range(4):
                sp.wait_ge(z["y"], 4 * q + 4)
                sp.dma_start(dram["out"][:, 4 * q:4 * q + 4], xsq[:, 4 * q:4 * q + 4]).then_inc(z["st"], 16)
            sp.wait_ge(z["st"], 64)

        @block.scalar
        def _(act):
            for t in range(KT):
                nc.scalar.activation(xsq[:, t], k.x[:, t], ACT.Square).then_inc(z["sq"], 1)
            act.wait_ge(z["ss"], 1)
            nc.scalar.activation(rstd[:], ss[:], ACT.Ln, bias=k.eps[:], scale=1.0 / D).then_inc(z["ln"], 1)
            act.wait_ge(z["ln"], 1)
            nc.scalar.activation(rstd[:], rstd[:], ACT.Exp, scale=-0.5).then_inc(z["rstd"], 1)

        @block.tensor
        def _(pe):
            for t in range(KT):
                pe.wait_ge(z["sq"], t + 1)
                last = nc.tensor.matmul(ss[:], k.ones[:], xsq[:, t], start=t == 0, stop=t == KT - 1)
            last.then_inc(z["ss"], 1)

        @block.vector
        def _(dve):
            dve.wait_ge(z["in"], 16)
            dve.wait_ge(z["rstd"], 1)
            for t in range(KT):
                nc.vector.scalar_tensor_tensor(xsq[:, t], k.x[:, t], fg[:, t:t + 1], rstd[:], ALU.mult, ALU.mult).then_inc(z["y"], 1)


class Shared:

    def __init__(self):
        self.semaphores = []

    def semaphore(self, nc, name):
        self.semaphores.append(nc.alloc_semaphore(name=name))
        return self.semaphores[-1]

    def clear_semaphores(self, nc):
        nc.all_engine_barrier()
        nc.clear_and_free_semaphores(self.semaphores)
        nc.all_engine_barrier()
        self.semaphores = []


def program(nc, dram):
    with ExitStack() as ctx:
        k = Shared()
        sb = lambda n, s, d=F32: ctx.enter_context(nc.sbuf_tensor(n, s, d))
        k.ident = sb("ident", [P, P])
        k.ones = sb("ones", [P, P])
        k.eps = sb("eps", [P, 1])
        k.c_act = sb("c_act", [P, KT, 2])
        k.mod2 = sb("mod2", [P, ADA - ADA1])
        with ExitStack() as c1:
            k.h_hi = c1.enter_context(nc.sbuf_tensor("h_hi", [P, KT, TOK], F32R))
            k.h_lo = c1.enter_context(nc.sbuf_tensor("h_lo", [P, KT, TOK], F32R))
            adaln_and_norm(nc, k, dram)
            input_projection(nc, k, dram)
        k.mix = k.q = sb("mix_then_query", [P, KT, SEQ])
        mixers(nc, k, dram)
        k.clear_semaphores(nc)
        k.x, k.a_hi, k.a_lo = sb("x", [P, KT, SEQ]), sb("h2_hi", [P, KT, SEQ], F32R), sb("h2_lo", [P, KT, SEQ], F32R)
        output_and_query(nc, k, dram)
        with ExitStack() as c1:
            k.picked = c1.enter_context(nc.sbuf_tensor("picked_t", [P, 3, SEQ], F32))
            retrieval(nc, k, dram)
            gate_matrix(nc, k, dram)
        experts(nc, k, dram)
        final_norm(nc, k, dram)


def columns(v, n):
    return np.ascontiguousarray(np.asarray(v).reshape(n, P).T)


def tiles(w):
    w = np.asarray(w)
    n = w.shape[1] // P
    return np.ascontiguousarray(w.reshape(KT, P, n, P).transpose(2, 1, 0, 3)).reshape(n, P, KT * P)


def groups_of_512(w):
    w = np.asarray(w)
    n = w.shape[1] // 512
    return np.ascontiguousarray(w.reshape(KT, P, n, 512).transpose(2, 1, 0, 3)).reshape(n, P, KT * 512)


def features(x):
    x = np.asarray(x)
    return np.ascontiguousarray(x.reshape(x.shape[0], KT, P).transpose(2, 1, 0))


def rope_tables():
    tok, feat = np.arange(SEQ), np.arange(P)
    n_freq = 16
    inv = 10000.0 ** (-np.arange(n_freq, dtype=np.float32) / n_freq)
    pos = np.where((feat % 64 < 32)[:, None], (tok // 64)[None, :], (tok % 64)[None, :]).astype(np.float32)
    ang = pos * inv.astype(np.float32)[feat % 16][:, None]
    first = feat % 32 < 16
    partner = np.where(first, feat + 16, feat - 16)
    perm = np.zeros((P, P), np.float32)
    perm[partner, feat] = 1.0
    sin = np.where(first[:, None], -np.sin(ang), np.sin(ang))
    return perm, np.cos(ang).astype(np.float32), sin.astype(np.float32)


def level_masks():
    s, t = np.arange(P)[:, None], np.arange(P)[None, :]
    out = [((s // (2 * L) == t // (2 * L)) & (s // L != t // L)) for L in (P >> (l + 1) for l in range(LEVELS))]
    return np.ascontiguousarray(np.stack(out, axis=1).astype(np.float32))


def layout(inputs):
    a = {}
    a["x"] = features(inputs["x"][0])
    a["ctx"] = features(inputs["ctx"][0])
    a["c"] = np.ascontiguousarray(np.stack([columns(inputs["c"][0], KT), columns(inputs["c_ctx"], KT)], axis=2))
    order = np.arange(ADA // 4)
    order[:ADA1 // 4] = order[:ADA1 // 4].reshape(2, KT // 4).T.reshape(-1)
    a["w_ada"] = groups_of_512(inputs["w_ada"][0])[order]
    a["b_ada"] = np.ascontiguousarray(columns(inputs["b_ada"][0], ADA).reshape(P, ADA // 4, 4)[:, order].reshape(P, ADA))
    a["norm1_g"] = columns(inputs["norm1_g"][0], KT)
    w_in = inputs["w_in"][0].reshape(D, 8, HEADS * P)[:, list(PART_OF)].reshape(D, 8 * HEADS * P)
    a["w_in"] = groups_of_512(w_in)
    a["ident"] = np.eye(P, dtype=np.float32)
    g = np.asarray(inputs["hg_gamma"])
    a["hg_gamma"] = np.ascontiguousarray(g.reshape(2, 2, HEADS, P).transpose(3, 0, 1, 2))
    a["hg_norm_g"] = columns(inputs["hg_norm_g"][0], HEADS)
    a["da_subln_g"] = columns(inputs["da_subln_g"][0], HEADS)
    a["da_lambda"] = np.stack([inputs["da_lambda_" + n][0] for n in ("q1", "q2", "k1", "k2")])[None]
    a["rope_perm"], a["rope_cos"], a["rope_sin"] = rope_tables()
    a["level_masks"] = level_masks()
    a["w_out"] = groups_of_512(inputs["w_out"][0])
    a["norm2_g"] = columns(inputs["norm2_g"][0], KT)
    a["w_query"] = groups_of_512(inputs["peer_w_query"][0])
    a["sub_keys"] = np.ascontiguousarray(np.asarray(inputs["peer_sub_keys"][0]).reshape(2 * HEADS, NKEYS, P).transpose(2, 0, 1))
    a["iota"] = np.tile(np.arange(NKEYS, dtype=np.float32), (P, 1))
    a["u"] = tiles(np.asarray(inputs["peer_u"][0]).T)
    a["v"] = np.asarray(inputs["peer_v"][0]).reshape(E_TILES, P, D)
    a["final_norm_g"] = columns(inputs["final_norm_g"], KT)
    return a


def kernel(**inputs):
    import concourse.bacc as bacc
    from concourse.bass_utils import run_bass_kernel_spmd

    nc = bacc.Bacc("TRN2", target_bir_lowering=False, num_devices=1)
    arrays = {f"in_{name}": a for name, a in layout(inputs).items()}
    dram = {name[3:]: nc.dram_tensor(name, a.shape, mybir.dt.from_np(a.dtype), kind="ExternalInput").ap() for name, a in arrays.items()}
    dram["out"] = nc.dram_tensor("y_features", (P, KT, SEQ), F32, kind="ExternalOutput").ap()
    for name, shape in (("proj_lat", (IN_TILES, P, SEQ)), ("proj_ctx", (5, CT, P, HEADS * P)), ("gate", (NKEYS, SEQ // TB, NKEYS, TB)),
                        ("act", (PAIR * EARLY, P, SEQ))):
        dram[name] = nc.dram_tensor(name, shape, F32, kind="Internal").ap()
    program(nc, dram)
    r = run_bass_kernel_spmd(nc, [arrays], core_ids=[0])
    y = np.asarray(r.results[0]["y_features"])
    return np.ascontiguousarray(y.transpose(2, 1, 0)).reshape(1, SEQ, D)
```
